# Optimizing a Trainium2 kernel written in Bass

```python
import jax, jax.numpy as jnp
from jax import lax
import numpy as np

D_MODEL = 1024
BATCH = 1
SEQ = 256
DEPTH = 1

CTX_LEN = 256
GRID_W = 64
SSD_EXPAND = 2
D_INNER = SSD_EXPAND * D_MODEL
SSD_HEAD_DIM = 64
SSD_HEADS = D_INNER // SSD_HEAD_DIM
SSD_GROUPS = 4
SSD_STATE = 128
SSD_CONV = 4
SSD_CHUNK = 128
SSD_GN = SSD_GROUPS * SSD_STATE
CONV_DIM = D_INNER + 2 * SSD_GN
SSD_PAD = ((SSD_CONV - 1) // 2, SSD_CONV // 2)
SC_WIDTH = D_MODEL
SC_CONV = 3
SC_PAD = ((SC_CONV - 1) // 2, SC_CONV // 2)
IN_WIDTHS = (D_INNER, CONV_DIM, 2 * SSD_HEADS, SC_WIDTH, SC_WIDTH, SC_WIDTH, D_MODEL, D_MODEL)
IN_COLS = sum(IN_WIDTHS)
N_EXPERTS = 16
N_EXPERT_GROUPS = 4
EXPERTS_PER_GROUP = N_EXPERTS // N_EXPERT_GROUPS
TOP_K = 2
D_EXPERT = 512
EPS = 1e-6

kernel_name = "hybrid_ssd_shortconv_moe_diffusion_trunk"

def rmsnorm(x, gain):
    xf = x.astype(jnp.float32)
    y = xf * lax.rsqrt(jnp.mean(xf * xf, axis=-1, keepdims=True) + EPS) * gain.astype(jnp.float32)
    return y.astype(x.dtype)

def modulate(h, gain, shift, scale):
    return rmsnorm(h, gain) * (1 + scale) + shift

def depthwise_conv(x, w, pad):
    return lax.conv_general_dilated(
        x, w[:, None, :].astype(x.dtype), window_strides=(1,), padding=[pad],
        dimension_numbers=("NWC", "WIO", "NWC"), feature_group_count=x.shape[-1])

def split_cols(p):
    idx = np.cumsum(np.array(IN_WIDTHS))[:-1].tolist()
    return jnp.split(p, idx, axis=-1)

def ssd_scan(x, dt, A, Bm, Cm, state0):
    b, L, H, P = x.shape
    G, N = Bm.shape[-2:]
    J = H // G
    nc = L // SSD_CHUNK
    f32 = jnp.float32

    def to_chunks(t):
        return jnp.moveaxis(t.reshape(b, nc, SSD_CHUNK, *t.shape[2:]), 1, 0)

    xs = to_chunks(x.astype(f32).reshape(b, L, G, J, P))
    dts = to_chunks(dt.astype(f32).reshape(b, L, G, J))
    Bs = to_chunks(Bm.astype(f32))
    Cs = to_chunks(Cm.astype(f32))
    Ag = A.astype(f32).reshape(G, J)
    lower = jnp.tril(jnp.ones((SSD_CHUNK, SSD_CHUNK), dtype=bool))[None, :, :, None, None]

    def step(state, inp):
        xc, dtc, Bc, Cc = inp
        a = jnp.cumsum(dtc * Ag, axis=1)
        seg = a[:, :, None] - a[:, None, :]
        decay = jnp.exp(jnp.where(lower, seg, -jnp.inf))
        cb = jnp.einsum("blgn,bsgn->blsg", Cc, Bc)
        xdt = xc * dtc[..., None]
        y_intra = jnp.einsum("blsg,blsgj,bsgjp->blgjp", cb, decay, xdt)
        y_inter = jnp.einsum("blgn,bgjpn->blgjp", Cc, state) * jnp.exp(a)[..., None]
        a_last = a[:, -1]
        w_in = jnp.exp(a_last[:, None] - a)[..., None]
        new_state = (state * jnp.exp(a_last)[..., None, None]
                     + jnp.einsum("bsgn,bsgjp->bgjpn", Bc, xdt * w_in))
        return new_state, y_intra + y_inter

    state, ys = lax.scan(step, state0.astype(f32).reshape(b, G, J, P, N), (xs, dts, Bs, Cs))
    y = jnp.moveaxis(ys, 0, 1).reshape(b, L, H, P)
    return y.astype(x.dtype), state.reshape(b, H, P, N)

def ssd_prep(xbc, dt_raw, conv_w, conv_b, dt_bias):
    b, L, _ = xbc.shape
    xbc = jax.nn.silu(depthwise_conv(xbc, conv_w, SSD_PAD) + conv_b)
    xs, bs, cs = jnp.split(xbc, [D_INNER, D_INNER + SSD_GN], axis=-1)
    dt = jax.nn.softplus(dt_raw.reshape(b, L, 2, SSD_HEADS).astype(jnp.float32)
                         + dt_bias.astype(jnp.float32))
    return (xs.reshape(b, L, SSD_HEADS, SSD_HEAD_DIM),
            bs.reshape(b, L, SSD_GROUPS, SSD_STATE),
            cs.reshape(b, L, SSD_GROUPS, SSD_STATE), dt)

def ssd_finish(y, xh, z, d_skip, gain, w_out):
    b, L = z.shape[:2]
    y = (y + xh * d_skip[:, None].astype(xh.dtype)).reshape(b, L, D_INNER)
    return rmsnorm(y * jax.nn.silu(z), gain) @ w_out

def short_conv(gb, gc, hv, conv_w, w_out, on_grid):
    v = gc * hv
    if on_grid:
        b, L, C = v.shape
        rows = L // GRID_W
        v = depthwise_conv(v.reshape(b * rows, GRID_W, C), conv_w, SC_PAD).reshape(b, L, C)
    else:
        v = depthwise_conv(v, conv_w, SC_PAD)
    return (gb * v) @ w_out

def merge(ga, gb, ya, yb, w_o):
    return (jax.nn.sigmoid(ga) * ya + jax.nn.sigmoid(gb) * yb) @ w_o

def hybrid_mixer(u, uc, w_in, conv_w, conv_b, dt_bias, a_log, d_skip, ssd_gain, w_ssd_out,
                 sc_w, w_sc_out, w_o, need_ctx):
    pl = split_cols(u @ w_in)
    pc = split_cols(uc @ w_in)
    xl, Bl, Cl, dtl = ssd_prep(pl[1], pl[2], conv_w, conv_b, dt_bias)
    xc, Bc, Cc, dtc = ssd_prep(pc[1], pc[2], conv_w, conv_b, dt_bias)
    A = -jnp.exp(a_log.astype(jnp.float32))
    zero = jnp.zeros((uc.shape[0], SSD_HEADS, SSD_HEAD_DIM, SSD_STATE), jnp.float32)

    def flip(t):
        return jnp.flip(t, axis=1)

    yc_f, s_f = ssd_scan(xc, dtc[:, :, 0], A[0], Bc, Cc, zero)
    yc_b, s_b = ssd_scan(flip(xc), flip(dtc[:, :, 1]), A[1], flip(Bc), flip(Cc), zero)
    yl_f, _ = ssd_scan(xl, dtl[:, :, 0], A[0], Bl, Cl, s_f)
    yl_b, _ = ssd_scan(flip(xl), flip(dtl[:, :, 1]), A[1], flip(Bl), flip(Cl), s_b)
    ssd_l = ssd_finish(yl_f + flip(yl_b), xl, pl[0], d_skip, ssd_gain, w_ssd_out)
    sc_l = short_conv(pl[3], pl[4], pl[5], sc_w, w_sc_out, True)
    out_l = merge(pl[6], pl[7], ssd_l, sc_l, w_o)
    if not need_ctx:
        return out_l, None
    ssd_c = ssd_finish(yc_f + flip(yc_b), xc, pc[0], d_skip, ssd_gain, w_ssd_out)
    sc_c = short_conv(pc[3], pc[4], pc[5], sc_w, w_sc_out, False)
    out_c = merge(pc[6], pc[7], ssd_c, sc_c, w_o)
    return out_l, out_c

def moe_ffn(u, w_router, b_router, w_gate, w_up, w_down):
    shp = u.shape
    t = u.reshape(-1, shp[-1])
    scores = jax.nn.sigmoid((t @ w_router).astype(jnp.float32))
    sel = scores + b_router.astype(jnp.float32)
    grouped = sel.reshape(-1, N_EXPERT_GROUPS, EXPERTS_PER_GROUP)
    group_score = lax.top_k(grouped, TOP_K)[0].sum(-1)
    best_group = jnp.argmax(group_score, axis=-1)
    in_group = (jnp.arange(N_EXPERTS) // EXPERTS_PER_GROUP)[None, :] == best_group[:, None]
    _, idx = lax.top_k(jnp.where(in_group, sel, -jnp.inf), TOP_K)
    w = jnp.take_along_axis(scores, idx, axis=-1)
    w = w / jnp.sum(w, axis=-1, keepdims=True)
    combine = jnp.einsum("tk,tke->te", w, jax.nn.one_hot(idx, N_EXPERTS, dtype=jnp.float32)).astype(u.dtype)
    out = jnp.zeros_like(t)
    for e in range(N_EXPERTS):
        hid = jax.nn.silu(t @ w_gate[e]) * (t @ w_up[e])
        out = out + combine[:, e:e + 1] * (hid @ w_down[e])
    return out.reshape(shp)

def setup_inputs(seed: int = 0) -> dict:
    key = jax.random.key(seed)
    ks = jax.random.split(key, 26)
    f32 = jnp.float32

    def nrm(k, shape, s):
        return jax.random.normal(k, shape, f32) * s

    dt0 = jnp.exp(jax.random.uniform(ks[11], (DEPTH, 2, SSD_HEADS), f32)
                  * (np.log(0.1) - np.log(0.001)) + np.log(0.001))
    return {
        "x": nrm(ks[0], (BATCH, SEQ, D_MODEL), 1.0),
        "c": nrm(ks[1], (BATCH, D_MODEL), 1.0),
        "ctx": nrm(ks[2], (BATCH, CTX_LEN, D_MODEL), 1.0),
        "c_ctx": nrm(ks[3], (D_MODEL,), 1.0),
        "w_ada": nrm(ks[4], (DEPTH, D_MODEL, 6 * D_MODEL), 0.5 * D_MODEL ** -0.5),
        "b_ada": nrm(ks[5], (DEPTH, 6 * D_MODEL), 0.01),
        "norm_mix": 1.0 + nrm(ks[6], (DEPTH, D_MODEL), 0.02),
        "norm_ffn": 1.0 + nrm(ks[7], (DEPTH, D_MODEL), 0.02),
        "w_in": nrm(ks[8], (DEPTH, D_MODEL, IN_COLS), D_MODEL ** -0.5),
        "ssd_conv_w": nrm(ks[9], (DEPTH, SSD_CONV, CONV_DIM), SSD_CONV ** -0.5),
        "ssd_conv_b": nrm(ks[10], (DEPTH, CONV_DIM), 0.01),
        "ssd_dt_bias": dt0 + jnp.log(-jnp.expm1(-dt0)),
        "ssd_a_log": jnp.log(jax.random.uniform(ks[12], (DEPTH, 2, SSD_HEADS), f32, 1.0, 16.0)),
        "ssd_d": 1.0 + nrm(ks[13], (DEPTH, SSD_HEADS), 0.1),
        "ssd_norm": 1.0 + nrm(ks[14], (DEPTH, D_INNER), 0.02),
        "w_ssd_out": nrm(ks[15], (DEPTH, D_INNER, D_MODEL), D_INNER ** -0.5),
        "sc_conv_w": nrm(ks[16], (DEPTH, SC_CONV, SC_WIDTH), SC_CONV ** -0.5),
        "w_sc_out": nrm(ks[17], (DEPTH, SC_WIDTH, D_MODEL), SC_WIDTH ** -0.5),
        "w_o": nrm(ks[18], (DEPTH, D_MODEL, D_MODEL), D_MODEL ** -0.5),
        "w_router": nrm(ks[19], (D_MODEL, N_EXPERTS), D_MODEL ** -0.5),
        "b_router": nrm(ks[20], (N_EXPERTS,), 0.01),
        "w_gate": nrm(ks[21], (DEPTH, N_EXPERTS, D_MODEL, D_EXPERT), D_MODEL ** -0.5),
        "w_up": nrm(ks[22], (DEPTH, N_EXPERTS, D_MODEL, D_EXPERT), D_MODEL ** -0.5),
        "w_down": nrm(ks[23], (DEPTH, N_EXPERTS, D_EXPERT, D_MODEL), D_EXPERT ** -0.5),
        "final_norm": 1.0 + nrm(ks[24], (D_MODEL,), 0.02),
    }

def reference(x, c, ctx, c_ctx, w_ada, b_ada, norm_mix, norm_ffn, w_in, ssd_conv_w, ssd_conv_b,
              ssd_dt_bias, ssd_a_log, ssd_d, ssd_norm, w_ssd_out, sc_conv_w, w_sc_out, w_o,
              w_router, b_router, w_gate, w_up, w_down, final_norm):
    h, hc = x, ctx
    n_ctx = ctx.shape[1]
    cond = jax.nn.silu(c)
    cond_ctx = jax.nn.silu(c_ctx)
    for l in range(DEPTH):
        last = l == DEPTH - 1
        m = jnp.split((cond @ w_ada[l] + b_ada[l])[:, None, :], 6, axis=-1)
        mc = jnp.split(cond_ctx @ w_ada[l] + b_ada[l], 6, axis=-1)
        u = modulate(h, norm_mix[l], m[0], m[1])
        uc = modulate(hc, norm_mix[l], mc[0], mc[1])
        y, yc = hybrid_mixer(u, uc, w_in[l], ssd_conv_w[l], ssd_conv_b[l], ssd_dt_bias[l], ssd_a_log[l],
                             ssd_d[l], ssd_norm[l], w_ssd_out[l], sc_conv_w[l], w_sc_out[l], w_o[l],
                             not last)
        h = h + m[2] * y
        if last:
            u2 = modulate(h, norm_ffn[l], m[3], m[4])
            h = h + m[5] * moe_ffn(u2, w_router, b_router, w_gate[l], w_up[l], w_down[l])
        else:
            hc = hc + mc[2] * yc
            u2 = jnp.concatenate([modulate(hc, norm_ffn[l], mc[3], mc[4]),
                                  modulate(h, norm_ffn[l], m[3], m[4])], axis=1)
            f = moe_ffn(u2, w_router, b_router, w_gate[l], w_up[l], w_down[l])
            hc = hc + mc[5] * f[:, :n_ctx]
            h = h + m[5] * f[:, n_ctx:]
    return rmsnorm(h, final_norm)


_drawn_inputs = setup_inputs


def setup_inputs(seed=0):
    import zlib

    import numpy as np

    out = dict(_drawn_inputs(seed))
    spreads = {}
    factors = {'ctx': 31.12,
     'c_ctx': 34.312,
     'norm_mix': 5.386,
     'norm_ffn': 24.712,
     'ssd_conv_b': 62.304,
     'ssd_norm': 50.504,
     'final_norm': 7.912,
     'ssd_dt_bias': 4.506,
     'ssd_a_log': 8.0,
     'ssd_d': 8.0,
     'b_router': 3.426}
    for name, (base, spread) in spreads.items():
        noise = np.random.default_rng([zlib.crc32(name.encode()), seed]).standard_normal(out[name].shape)
        drawn = base * np.exp(spread * noise) if base else spread * noise
        out[name] = __import__('jax').numpy.asarray(drawn.astype(out[name].dtype))
    for name, factor in factors.items():
        out[name] = (out[name] * factor).astype(out[name].dtype)
    return out
```

```python
from contextlib import ExitStack

import concourse.bass as bass
from concourse import mybir

F32 = mybir.dt.float32
F32R = mybir.dt.float32r
I32 = mybir.dt.int32
ALU = mybir.AluOpType
ACT = mybir.ActivationFunctionType
AX_X = mybir.AxisListType.X

P = 128
D = 1024
KD = D // P
T = 256
TB = T // P
INNER = 2048
HEADS = 32
GROUPS = 4
NE = 16
EPS = 1e-6

U_DT = 0
U_B = 1
U_C = 5
U_X = 9
U_Z = 25
U_CH = 41
U_GATEB = 57
U_MB = 65
U_MA = 73
U_SC = 81
U_SSD = 89
U_O = 105
U_END = 113
RAW = 4

C_COND, C_BADA, C_NMIX, C_CW, C_CB, C_SSDN, C_SCW, C_DSKIP, C_IDENT = 0, 16, 32, 40, 136, 160, 176, 200, 216
C_ONES, C_UP, C_LO, C_IOTA, C_TRI, C_NTRI, C_END = 344, 472, 600, 728, 856, 872, 888

DT_AT = [0, 4, 8, 12, 14, 18, 22, 30]
DT_REV, DT_DONE = 30, 31
LOG1P = [1.0 / (2 * j + 1) for j in range(8)]


def first_unit_of_step(s):
    return U_CH + min(s, 32) * 40 // 32


def build(nc, a, out, scratch):
    with ExitStack() as ctx:
        base = 16512
        ctx.enter_context(nc.sbuf_tensor("arena", [P, 53000], F32))

        def at(name, kib, shape, dt=F32):
            return nc.alloc_sbuf_tensor_at(name, shape, dt, offset=base + int(kib * 1024))

        def sem(name):
            return ctx.enter_context(nc.semaphore(name))

        ps = [ctx.enter_context(nc.psum_tensor(f"ps{i}", [P, 512], F32)) for i in range(8)]

        par = at("par", 0, [P, C_END])
        headrow = at("headrow", 3.5, [64, 2])
        a_pos = at("a_pos", 3.75, [64, 1])
        u_hi = at("u_hi", 4, [P, 2, KD, T], F32R)
        u_lo = at("u_lo", 20, [P, 2, KD, T], F32R)
        raw = at("raw", 36, [P, RAW, KD, P])
        w_hi = [at(f"w_hi{i}", 52 + 4 * i, [P, KD, P], F32R) for i in range(2)]
        w_lo = [at(f"w_lo{i}", 60 + 4 * i, [P, KD, P], F32R) for i in range(2)]
        x_in = at("x_in", 108, [P, KD, 2 * T])
        x_sq = at("x_sq", 148, [P, KD, 2 * T])
        mean_sq = at("mean_sq", 132, [P, 2 * T])
        rms_in = at("rms_in", 134, [P, 2 * T])
        rstd_in = at("rstd_in", 136, [P, 2 * T])
        cond = at("cond", 138, [P, KD, 2])
        mod_col = at("mod_col", 138.25, [P, 16, 2])
        gain_col = at("gain_col", 138.5, [P, KD, 2])
        mod_row = at("mod_row", 68, [2, 2048])
        wa = [at("wa0", 92, [P, KD, 512]), at("wa1", 168, [P, KD, 512])]
        ada_sum = at("ada_sum", 132, [P, 8, 512])
        cond_keep = at("cond_keep", 204, [P, KD])
        ada_row = at("ada_row", 92, [1, 4096])
        conv = [at(f"conv{i}", 88 + 2 * i, [P, 2, T]) for i in range(2)]
        dt_r = at("dt_r", 76, [64, 512])
        dt_e = at("dt_e", 78, [64, 512])
        dt_t = at("dt_t", 80, [64, 512])
        dt_t2 = at("dt_t2", 82, [64, 512])
        dt_q = at("dt_q", 84, [64, 512])
        dt = at("dt", 86, [64, 4, P])
        rev = at("rev", 68, [64, 4, P])
        w_ctx = at("w_ctx", 70, [64, 2, P])
        dec_t = at("dec_t", 71, [64, 2, P])
        coef_t = at("coef_t", 72, [64, 2, P])
        cum = at("cum", 187.5, [64, 4, P])
        tok = at("tok", 185, [P, 2, 4, 64])
        coef = at("coef", 187, [P, 2, 64])
        vc = at("vc", 68, [P, KD, T])
        v_tmp = [at(f"v_tmp{i}", 202 + i, [P, T]) for i in range(2)]
        gb_hi = at("gb_hi", 4, [P, KD, T], F32R)
        gb_lo = at("gb_lo", 20, [P, KD, T], F32R)
        gb_tmp = [at(f"gb_tmp{i}", 204.25 + i, [P, T]) for i in range(2)]
        m_a = at("m_a", 76, [P, KD, T])
        m_b = at("m_b", 84, [P, KD, T])
        z = at("z", 92, [P, 16, T])
        xl = at("xl", 108, [P, 16, T])
        bl = at("bl", 124, [P, GROUPS, T])
        cl = at("cl", 128, [P, GROUPS, T])
        xc = at("xc", 148, [P, 16, T])
        bc = at("bc", 164, [P, GROUPS, T])
        state = at("state", 132, [P, GROUPS, 2, 512])
        xw = at("xw", 190, [P, 2, 2, 512])
        b_tok = at("b_tok", 198, [P, 2 * GROUPS, P])
        xn = [at(f"xn{i}", 148 + 4 * i, [P, 2, 512]) for i in range(2)]
        cb_up = [at(f"cb_up{i}", 156 + 3 * i, [P, 2, P]) for i in range(2)]
        cb_lo = [at(f"cb_lo{i}", 157 + 3 * i, [P, 2, P]) for i in range(2)]
        cb_off = [at(f"cb_off{i}", 158 + 3 * i, [P, 2, P]) for i in range(2)]
        yi = [at(f"yi{i}", 162 + 4 * i, [P, 2, 512]) for i in range(2)]
        yi_tmp = at("yi_tmp", 170, [P, 512])
        back = at("back", 172, [P, 2, P])
        expo = at("expo", 173, [P, 2, P])
        dec = [at(f"dec{i}", 174 + 2 * i, [P, 4, P]) for i in range(2)]
        wd_tmp = at("wd_tmp", 178, [P, 2, P])
        wd = [at(f"wd{i}", 179 + i, [P, 2, P]) for i in range(2)]
        mix = [at(f"mix{i}", 181 + 2 * i, [P, 4, P]) for i in range(2)]

        sq2 = at("sq2", 148, [P, 16, T])
        gg_hi = at("gg_hi", 92, [P, 16, T], F32R)
        gg_lo = at("gg_lo", 132, [P, 16, T], F32R)
        m_hi = at("m_hi", 164, [P, KD, T], F32R)
        m_lo = at("m_lo", 172, [P, KD, T], F32R)
        merged = [at(f"merged{i}", 180 + i, [P, T]) for i in range(2)]
        rstd2 = at("rstd2", 182, [P, T])
        rms2 = at("rms2", 183, [P, T])
        b_row = at("b_row", 168, [1, 4096])
        mod_rest = at("mod_rest", 108, [P, 4, D])
        norm_rows = at("norm_rows", 124, [P, 2, D])
        x_nat = at("x_nat", 68, [P, TB, D])
        h = at("h", 12, [P, TB, D])
        u2 = at("u2", 28, [P, TB, D])
        u2_hi = at("u2_hi", 4, [P, TB, D], F32R)
        u2_lo = at("u2_lo", 20, [P, TB, D], F32R)
        u2_t = at("u2_t", 76, [P, KD, T])
        w_rt = at("w_rt", 196, [P, KD, NE])
        b_rt = at("b_rt", 196.5, [P, NE])
        stat = at("stat", 196.75, [P, 8])
        n_iter = at("n_iter", 196.8125, [1, 2], I32)
        cmp_gt = at("cmp_gt", 197, [P, 8, 4, 4])
        cmp_ge = at("cmp_ge", 197.5, [P, 8, 4, 4])
        score = at("score", 198, [P, TB, NE])
        sel = at("sel", 198.125, [P, TB, NE])
        rank = at("rank", 198.25, [P, 8, 4])
        top2 = at("top2", 198.375, [P, 8, 4])
        g_score = at("g_score", 198.5, [P, 8])
        g_rank = at("g_rank", 198.5625, [P, 8])
        chosen = at("chosen", 198.625, [P, TB, NE])
        comb = at("comb", 198.75, [P, TB, NE])
        slot = at("slot", 198.875, [P, TB, NE])
        sel_top = at("sel_top", 199, [P, 8, 4])
        slots = at("slots", 199.25, [P, 17, TB, 2])
        combs = at("combs", 199.75, [P, 16, TB, 2])
        comb_slot = at("comb_slot", 200.25, [P, 2])
        ex_raw = [at(f"ex_raw{i}", 132 + 16 * i, [P, KD, 512]) for i in range(3)]
        ex_hi = [at(f"ex_hi{i}", 36 + 4 * i, [P, 2, 512], F32R) for i in range(4)]
        ex_lo = [at(f"ex_lo{i}", 52 + 4 * i, [P, 2, 512], F32R) for i in range(4)]
        xg_hi = at("xg_hi", 76, [P, KD, 2 * P], F32R)
        xg_lo = at("xg_lo", 84, [P, KD, 2 * P], F32R)
        y_hi = at("y_hi", 92, [P, D], F32R)
        y_lo = at("y_lo", 96, [P, D], F32R)
        pick = at("pick", 100, [P, TB, 2, P], F32R)
        put = at("put", 102, [P, 2, TB, P], F32R)
        act_g = at("act_g", 104, [P, 512])
        hid = at("hid", 106, [P, 512])
        hid_hi = at("hid_hi", 68, [P, 4, P], F32R)
        hid_lo = at("hid_lo", 70, [P, 4, P], F32R)
        zero_r = at("zero_r", 72, [P, 512], F32R)
        result = at("result", 28, [P, TB, D])

        def c_(i, n=1):
            return par[:, i:i + n]

        ident = c_(C_IDENT, P)
        ones = c_(C_ONES, P)

        par_in = sem("par_in")
        x_loaded = sem("x_loaded")
        headrow_in = sem("headrow_in")
        raw_full = [sem(f"raw_full{i}") for i in range(RAW)]
        wa_full = [sem(f"wa_full{i}") for i in range(2)]
        cond_ready = sem("cond_ready")
        sq_ready = sem("sq_ready")
        ms_done = sem("ms_done")
        ms_read = sem("ms_read")
        rms_ready = sem("rms_ready")
        xn_chain = sem("xn_chain")
        ada_mm = sem("ada_mm")
        mod_row_ready = sem("mod_row_ready")
        mod_tp = sem("mod_tp")
        mod_ready = sem("mod_ready")
        u_f = sem("u_f")
        u_hi_ready = sem("u_hi_ready")
        u_lo_ready = sem("u_lo_ready")
        split_hi = sem("split_hi")
        split_lo = sem("split_lo")
        unit_done = sem("unit_done")
        dt_read = sem("dt_read")
        copied = sem("copied")
        v_made = sem("v_made")
        gated = sem("gated")
        gb_hi_ready = sem("gb_hi_ready")
        gb_lo_ready = sem("gb_lo_ready")
        carry_chain = sem("carry_chain")
        wd_ready = sem("wd_ready")
        conv_init = sem("conv_init")
        conv_tap = sem("conv_tap")
        conv_done = sem("conv_done")
        act_dt = sem("act_dt")
        dve_dt = sem("dve_dt")
        ada_acc = sem("ada_acc")
        ada_summed = sem("ada_summed")
        ada_row_ready = sem("ada_row_ready")
        ada_stored = sem("ada_stored")
        piece = sem("piece")
        piece_act = sem("piece_act")
        piece_dve = sem("piece_dve")
        v_chain = sem("v_chain")
        rows_done = sem("rows_done")
        expo_ready = sem("expo_ready")
        scan_chain = sem("scan_chain")
        dec_ready = sem("dec_ready")
        mix_ready = sem("mix_ready")
        y_done = sem("y_done")
        y_stored = sem("y_stored")
        b_row_in = sem("b_row_in")
        sig_ready = sem("sig_ready")
        z_act = sem("z_act")
        gy_made = sem("gy_made")
        sq2_made = sem("sq2_made")
        ssq_done = sem("ssq_done")
        ms2_ready = sem("ms2_ready")
        rms2_ready = sem("rms2_ready")
        ma_scaled = sem("ma_scaled")
        gg_hi_ready = sem("gg_hi_ready")
        gg_lo_ready = sem("gg_lo_ready")
        branch_b = sem("branch_b")
        merge_chain = sem("merge_chain")
        merge_made = sem("merge_made")
        m_hi_ready = sem("m_hi_ready")
        m_lo_ready = sem("m_lo_ready")
        mod_rest_in = sem("mod_rest_in")
        norm_rows_in = sem("norm_rows_in")
        x_nat_in = sem("x_nat_in")
        w_rt_in = sem("w_rt_in")
        b_rt_in = sem("b_rt_in")
        nf_made = sem("nf_made")
        h_chain = sem("h_chain")
        h_sq = sem("h_sq")
        h_ms = sem("h_ms")
        h_rms = sem("h_rms")
        u2_chain = sem("u2_chain")
        u2_hi_ready = sem("u2_hi_ready")
        u2_lo_ready = sem("u2_lo_ready")
        u2_tp = sem("u2_tp")
        u2_t_act = sem("u2_t_act")
        u2_t_dve = sem("u2_t_dve")
        logits_done = sem("logits_done")
        score_ready = sem("score_ready")
        route = sem("route")
        positions = sem("positions")
        ex_full = [sem(f"ex_full{i}") for i in range(3)]
        ex_hi_ready = sem("ex_hi_ready")
        ex_lo_ready = sem("ex_lo_ready")
        ex_done = sem("ex_done")
        zeros_made = sem("zeros_made")
        acc_started = sem("acc_started")
        pick_ready = sem("pick_ready")
        gathered = sem("gathered")
        xg_hi_ready = sem("xg_hi_ready")
        xg_lo_ready = sem("xg_lo_ready")
        act_g_ready = sem("act_g_ready")
        hid_ready = sem("hid_ready")
        hid_tp = sem("hid_tp")
        hid_hi_ready = sem("hid_hi_ready")
        hid_lo_ready = sem("hid_lo_ready")
        put_tp = sem("put_tp")
        put_ready = sem("put_ready")
        comb_mm = sem("comb_mm")
        comb_ready = sem("comb_ready")
        y_hi_ready = sem("y_hi_ready")
        y_lo_ready = sem("y_lo_ready")
        scattered = sem("scattered")
        moe_done = sem("moe_done")
        fin = sem("fin")
        fin_sq = sem("fin_sq")
        fin_rms = sem("fin_rms")
        out_stored = sem("out_stored")

        def freed(u):
            if u == U_DT:
                return dt_read, 1
            if u < U_Z:
                return conv_tap, 3 * (u - U_B) + 3
            if u < U_CH:
                return copied, u - U_Z + 1
            if u < U_GATEB:
                i = (u - U_CH) // 2
                return (copied, 16 + i + 1) if (u - U_CH) % 2 == 0 else (v_made, i + 1)
            if u < U_MB:
                return gated, u - U_GATEB + 1
            if u < U_SC:
                return copied, 24 + (u - U_MB) + 1
            return branch_b, u - U_SC + 1

        PIECES = [("tables", 0), ("b_ctx", 0)]
        for g in range(GROUPS):
            PIECES += [("x_ctx", g), ("state", g)]
        for g in range(GROUPS):
            PIECES += [("x_lat", g), ("cb", g), ("carry", 2 * g), ("carry", 2 * g + 1)]
        BY_ACT = ("tables", "b_ctx", "state", "x_lat", "cb")
        BY_DVE = ("tables", "x_ctx", "cb", "carry")

        def act_pieces(n):
            return sum(k in BY_ACT for k, _ in PIECES[:n])

        def dve_pieces(n):
            return sum(k in BY_DVE for k, _ in PIECES[:n])

        FIRST_PIECE_UNIT = U_Z + 1

        def piece_at_unit(u):
            n = u - FIRST_PIECE_UNIT
            return n if 0 <= n < 14 else None

        def piece_at_step(s):
            g, k = s // 8, s % 8 - 1
            return 10 + 4 * (g + 1) + k if g < GROUPS - 1 and 0 <= k < 4 else None

        ROUTE_CHOSEN, ROUTE_SLOTS, ROUTE_N = 18, 27, 31
        FIN_OUT = 11

        block = ctx.enter_context(nc.Block())

        @block.sync
        def _(sp):
            sp.dma_start(par[:, :], a["par"]).then_inc(par_in, 16)
            sp.dma_start(x_in[:, :, :], a["x_t"]).then_inc(x_loaded, 16)
            sp.dma_start(headrow[:, :], a["head_rows"]).then_inc(headrow_in, 16)
            n_wa = 0

            def load_wa(j):
                if 2 <= j < 6:
                    sp.wait_ge(ada_mm, j - 1)
                if j >= 6:
                    sp.wait_ge(ada_acc, 8 * (j - 5))
                sp.dma_start(wa[j % 2][:, :, :], a["w_ada"][j]).then_inc(wa_full[j % 2], 16)

            def load_unit(u):
                if u >= RAW:
                    sp.wait_ge(split_lo, u - RAW + 1)
                if u == U_DT:
                    sp.dma_start(raw[:, 0, :, 0:64], a["w_dt"]).then_inc(raw_full[0], 16)
                else:
                    sp.dma_start(raw[:, u % RAW, :, :], a["units"][u - 1]).then_inc(raw_full[u % RAW], 16)

            for j in range(4):
                load_wa(j)
            for u in range(RAW):
                load_unit(u)
            for j in range(4, 6):
                load_wa(j)
            for u in range(RAW, U_SC):
                load_unit(u)
                if u >= 6 and (u - 6) % 2 == 0 and (u - 6) // 2 < 6:
                    load_wa(6 + (u - 6) // 2)
                if u == U_Z - 1:
                    sp.wait_ge(ada_acc, 64)
                    sp.dma_start(b_row[:, :], a["b_ada_rest"]).then_inc(b_row_in, 16)
                if u == U_Z + 2:
                    sp.wait_ge(ada_row_ready, 8)
                    sp.dma_start(scratch, ada_row[:, :]).then_inc(ada_stored, 16)
            for u in range(U_SC, U_END):
                load_unit(u)
                if u == U_SC + 3:
                    sp.wait_ge(y_done, HEADS)
                    sp.wait_ge(gb_lo_ready, KD)
                    sp.dma_start(norm_rows[:, :, :], a["rows"].unsqueeze(0).to_broadcast([P, 2, D])).then_inc(norm_rows_in, 16)
                    sp.dma_start(x_nat[:, :, :], a["x"].rearrange("(b p) d -> p b d", p=P)).then_inc(x_nat_in, 16)
                    sp.dma_start(w_rt[:, :, :], a["w_router"]).then_inc(w_rt_in, 16)
                    sp.dma_start(b_rt[:, :], a["b_router"].to_broadcast([P, NE])).then_inc(b_rt_in, 16)
                if u == U_SSD + 4:
                    sp.wait_ge(ada_stored, 16)
                    sp.wait_ge(sq2_made, 4)
                    sp.wait_ge(gg_lo_ready, 16)
                    sp.dma_start(mod_rest[:, :, :], scratch.rearrange("a (k d) -> a k d", k=4).to_broadcast([P, 4, D]))\
                      .then_inc(mod_rest_in, 16)

            def load_expert(x, index):
                for m in range(3):
                    sp.wait_ge(ex_lo_ready, 12 * x + 4 * m + 4)
                    sp.dma_start(ex_raw[m][:, :, :], a["experts"][3 * index + m]).then_inc(ex_full[m], 16)

            for m in range(3):
                if m == 0:
                    sp.wait_ge(unit_done, U_O)
                elif m == 1:
                    sp.wait_ge(ssq_done, 1)
                else:
                    sp.wait_ge(unit_done, U_END)
                sp.dma_start(ex_raw[m][:, :, :], a["experts"][m]).then_inc(ex_full[m], 16)
            with sp.Fori(0, 7) as pair:
                load_expert(2 * pair + 1, 2 * pair + 1)
                load_expert(2 * pair + 2, 2 * pair + 2)
            load_expert(15, 15)
            sp.wait_ge(route, ROUTE_N)
            n = sp.value_load(n_iter[0:1, 0:1], min_val=8, max_val=16)
            with sp.If(n > 8):
                with sp.Fori(0, 8) as pair:
                    load_expert(2 * pair + 16, 2 * pair)
                    load_expert(2 * pair + 17, 2 * pair + 1)
            for b in range(TB):
                sp.wait_ge(fin, FIN_OUT + b)
                sp.dma_start(out[b * P:(b + 1) * P, :], result[:, b, :]).then_inc(out_stored, 16)
            sp.wait_ge(out_stored, 16 * TB)

        @block.tensor
        def _(pe):
            pe.wait_ge(par_in, 16)
            pe.wait_ge(sq_ready, 1)
            for k in range(KD):
                mm = pe.matmul(ps[0][:, :], ones, x_sq[:, k, :], start=k == 0, stop=k == KD - 1)
            mm.then_inc(ms_done, 1)
            pe.wait_ge(cond_ready, 1)
            for j in range(4):
                pe.wait_ge(wa_full[j % 2], 16 * (j // 2 + 1))
                for k in range(KD):
                    mm = pe.matmul(ps[1 + j][0:2, :], cond[:, k, :], wa[j % 2][:, k, :],
                                   start=k == 0, stop=k == KD - 1)
                mm.then_inc(ada_mm, 1)
            pe.wait_ge(mod_row_ready, 4)
            for t in range(16):
                mm = pe.transpose(ps[5][:, 2 * t:2 * t + 2], mod_row[0:2, t * P:(t + 1) * P], par[0:2, C_IDENT:C_IDENT + 2])
            mm.then_inc(mod_tp, 1)

            def unit(u, out_ap, hi, lo, first=True, last=True, m=P):
                pe.wait_ge(split_hi, u + 1)
                wh, wl = w_hi[u % 2], w_lo[u % 2]
                for k in range(KD):
                    pe.matmul(out_ap, wh[:, k, 0:m], hi(k), start=first and k == 0, stop=False)
                    pe.matmul(out_ap, wh[:, k, 0:m], lo(k), start=False, stop=False)
                pe.wait_ge(split_lo, u + 1)
                for k in range(KD):
                    mm = pe.matmul(out_ap, wl[:, k, 0:m], hi(k), start=False, stop=last and k == KD - 1)
                mm.then_inc(unit_done, 1)

            def in_unit(u):
                if u == 0:
                    pe.wait_ge(ms_read, 1)
                    pe.wait_ge(u_hi_ready, KD)
                    pe.wait_ge(u_lo_ready, KD)
                if u >= 2:
                    pe.wait_ge(*freed(u - 2))
                bank = ps[u % 2]
                if u == U_DT:
                    unit(u, bank[0:64, :], lambda k: u_hi[:, :, k, :], lambda k: u_lo[:, :, k, :], m=64)
                elif U_C <= u < U_X or u >= U_Z:
                    unit(u, bank[:, 0:T], lambda k: u_hi[:, 1, k, :], lambda k: u_lo[:, 1, k, :])
                else:
                    unit(u, bank[:, :], lambda k: u_hi[:, :, k, :], lambda k: u_lo[:, :, k, :])

            def transposes(bank, cols, src):
                for i, s in enumerate(src):
                    mm = pe.transpose(bank[:, i * cols:(i + 1) * cols], s, par[0:cols, C_IDENT:C_IDENT + cols])
                return mm

            def run_piece(n):
                kind, g = PIECES[n]
                if n and act_pieces(n):
                    pe.wait_ge(piece_act, act_pieces(n))
                if n and dve_pieces(n):
                    pe.wait_ge(piece_dve, dve_pieces(n))
                b6, b7 = ps[6], ps[7]
                if kind == "tables":
                    pe.wait_ge(dve_dt, DT_DONE)
                    pe.wait_ge(act_dt, 8)
                    src = []
                    for b in range(2):
                        src += [cum[:, 2 + b, :], dt[:, 2 + b, :], rev[:, 2 + b, :], dec_t[:, b, :]]
                    transposes(b6, 64, src)
                    mm = transposes(b7, 64, [coef_t[:, b, :] for b in range(2)])
                elif kind == "b_ctx":
                    pe.wait_ge(conv_done, 24)
                    transposes(b6, P, [bc[:, i // 2, (i % 2) * P:(i % 2 + 1) * P] for i in range(4)])
                    mm = transposes(b7, P, [bc[:, i // 2, (i % 2) * P:(i % 2 + 1) * P] for i in range(4, 8)])
                elif kind == "x_ctx":
                    for b in range(2):
                        mm = transposes(ps[6 + b], P, [xc[:, 4 * g + t, b * P:(b + 1) * P] for t in range(4)])
                elif kind == "state":
                    for d in range(2):
                        for b in range(2):
                            mm = pe.matmul(ps[6 + d][:, :], b_tok[:, 2 * g + b, :], xw[:, b, d, :],
                                           start=b == 0, stop=b == 1)
                elif kind == "x_lat":
                    for b in range(2):
                        mm = transposes(ps[6 + b], P, [xl[:, 4 * g + t, b * P:(b + 1) * P] for t in range(4)])
                elif kind == "cb":
                    for i, (s, l) in enumerate(((0, 0), (0, 1), (1, 1), (1, 0))):
                        mm = pe.matmul(b7[:, i * P:(i + 1) * P], bl[:, g, s * P:(s + 1) * P], cl[:, g, l * P:(l + 1) * P],
                                       start=True, stop=True)
                else:
                    gg, l = g // 2, g % 2
                    for d in range(2):
                        mm = pe.matmul(ps[6 + d][:, :], cl[:, gg, l * P:(l + 1) * P], state[:, gg, d, :],
                                       start=True, stop=True)
                mm.then_inc(piece, 1)

            def sum_ada():
                for j in range(8):
                    pe.wait_ge(ada_acc, 8 * j + 8)
                    if j >= 2:
                        pe.wait_ge(ada_row_ready, j - 1)
                    pe.matmul(ps[2 + j % 2][0:1, :], ones[:, 0:1], ada_sum[:, j, :],
                              start=True, stop=True).then_inc(ada_summed, 1)

            for u in range(U_CH):
                in_unit(u)
                if u == U_Z - 1:
                    sum_ada()
                if piece_at_unit(u) is not None:
                    run_piece(piece_at_unit(u))

            def head_rows(h):
                if h == 0:
                    pe.wait_ge(ada_row_ready, 8)
                if h >= 2:
                    pe.wait_ge(dec_ready, h - 1)
                for d in range(2):
                    mm = pe.matmul(ps[2 + h % 2][:, d * T:(d + 1) * T],
                                   par[0:64, C_IDENT + 32 * d + h:C_IDENT + 32 * d + h + 1].to_broadcast([64, P]),
                                   cum[:, 2:4, :], start=d == 0, stop=d == 1, skip_group_check=True)
                mm.then_inc(rows_done, 1)

            def y_head(h):
                g, pair, j = h // 8, h // 2, h % 2
                bank = ps[4 + pair % 2]
                if j == 0:
                    if pair >= 2:
                        pe.wait_ge(y_stored, pair - 1)
                    n = 10 + 4 * (g + 1)
                    pe.wait_ge(piece_dve, dve_pieces(n))
                    pe.wait_ge(piece_act, act_pieces(n))
                    for l in range(2):
                        pe.matmul(bank[:, l * P:(l + 1) * P], yi[g % 2][:, l, (pair % 4) * P:(pair % 4 + 1) * P], ident,
                                  start=l == 0, stop=False, skip_group_check=True)
                pe.wait_ge(mix_ready, h + 1)
                hh = h % 8
                for b in range(2):
                    mm = pe.matmul(bank[64 * j:64 * j + 64, 0:T], xn[g % 2][:, b, 64 * hh:64 * hh + 64],
                                   mix[h % 2][:, 2 * b:2 * b + 2, :], start=False, stop=j == 1 and b == 1,
                                   skip_group_check=True)
                mm.then_inc(y_done, 1)

            for s in range(HEADS + 2):
                if s < HEADS:
                    head_rows(s)
                for u in range(first_unit_of_step(s), first_unit_of_step(s + 1)):
                    in_unit(u)
                if s >= 2:
                    y_head(s - 2)
                if piece_at_step(s) is not None:
                    run_piece(piece_at_step(s))

            pe.wait_ge(gb_lo_ready, KD)
            for u in range(U_SC, U_SSD):
                pe.wait_ge(*freed(u - 2))
                unit(u, ps[u % 2][:, 0:T], lambda k: gb_hi[:, k, :], lambda k: gb_lo[:, k, :])
            pe.wait_ge(sq2_made, 4)
            for t in range(16):
                mm = pe.matmul(ps[6][:, 0:T], ones, sq2[:, t, :], start=t == 0, stop=t == 15)
            mm.then_inc(ssq_done, 1)
            pe.wait_ge(gg_lo_ready, 16)
            pe.wait_ge(branch_b, KD)
            for n in range(KD):
                if n >= 2:
                    pe.wait_ge(merge_made, n - 1)
                for half in range(2):
                    unit(U_SSD + 2 * n + half, ps[n % 2][:, 0:T], lambda k: gg_hi[:, 8 * half + k, :],
                         lambda k: gg_lo[:, 8 * half + k, :], first=half == 0, last=half == 1)
            pe.wait_ge(y_stored, 16)
            for k in range(KD):
                u = U_O + k
                pe.wait_ge(m_lo_ready, k + 1)
                pe.wait_ge(split_hi, u + 1)
                pe.wait_ge(split_lo, u + 1)
                for b in range(TB):
                    for half in range(2):
                        bank = ps[2 + 2 * b + half][:, :]
                        wh, wl = (w[u % 2][:, 4 * half:4 * half + 4, :] for w in (w_hi, w_lo))
                        mh, ml = (m[:, k, b * P:(b + 1) * P] for m in (m_hi, m_lo))
                        pe.matmul(bank, mh, wh, start=k == 0, stop=False)
                        pe.matmul(bank, ml, wh, start=False, stop=False)
                        mm = pe.matmul(bank, mh, wl, start=False, stop=k == KD - 1)
                mm.then_inc(unit_done, 1)
            pe.sem_inc(ex_done, 4)
            pe.sem_inc(scattered, 1)
            pe.wait_ge(merge_made, KD)
            for b in range(TB):
                pe.wait_ge(u2_chain, 2 * b + 2)
                for i in range(4):
                    for j in range(2):
                        k = 2 * i + j
                        mm = pe.transpose(ps[(0, 1, 6, 7)[i]][:, (2 * j + b) * P:(2 * j + b + 1) * P],
                                          u2[:, b, k * P:(k + 1) * P], ident)
            mm.then_inc(u2_tp, 1)
            pe.wait_ge(u2_t_act, 1)
            pe.wait_ge(u2_t_dve, 1)
            pe.wait_ge(w_rt_in, 16)
            for b in range(TB):
                for k in range(KD):
                    mm = pe.matmul(ps[2][:, b * NE:(b + 1) * NE], u2_t[:, k, b * P:(b + 1) * P], w_rt[:, k, :],
                                   start=k == 0, stop=k == KD - 1)
            mm.then_inc(logits_done, 1)
            pe.wait_ge(route, ROUTE_CHOSEN)
            up = c_(C_UP, P)
            pe.matmul(ps[3][:, 0:NE], up, chosen[:, 0, :], start=True, stop=True)
            for o, second in ((NE, up), (2 * NE, ones)):
                pe.matmul(ps[3][:, o:o + NE], ones, chosen[:, 0, :], start=True, stop=False)
                mm = pe.matmul(ps[3][:, o:o + NE], second, chosen[:, 1, :], start=False, stop=True)
            mm.then_inc(positions, 1)

            def gather(first):
                for r in range(4):
                    bank = ps[(7, 4, 5, 4)[r]]
                    if r == 3:
                        pe.wait_ge(xg_lo_ready, first + 2)
                    for j in range(2):
                        k = 2 * r + j
                        for n_mm, (x, b) in enumerate(((u2_hi, 0), (u2_hi, 1), (u2_lo, 0), (u2_lo, 1))):
                            mm = pe.matmul(bank[:, j * 2 * P:(j + 1) * 2 * P], x[:, b, k * P:(k + 1) * P], pick[:, b, :, :],
                                           start=n_mm == 0, stop=n_mm == 3)
                    mm.then_inc(gathered, 1)

            def scatter(put_e, after):
                pe.wait_ge(y_lo_ready, after)
                for b in range(TB):
                    for half in range(2):
                        for y in (y_hi, y_lo):
                            mm = pe.matmul(ps[2 * b + half][:, :], put[:, put_e, b, :], y[:, half * 512:(half + 1) * 512],
                                           start=False, stop=False, skip_group_check=True)
                mm.then_inc(scattered, 1)

            pe.wait_ge(zeros_made, 1)
            pe.wait_ge(route, ROUTE_N)
            zr = zero_r[:, 0:P]
            for i in (0, 1, 2, 3, 6):
                mm = pe.matmul(ps[i][:, :], zr, zero_r[:, :], start=True, stop=i > 3, skip_group_check=i <= 3)
            mm.then_inc(acc_started, 1)
            pe.wait_ge(u2_hi_ready, TB)
            pe.wait_ge(u2_lo_ready, TB)
            pe.wait_ge(pick_ready, 1)
            gather(0)
            n = pe.value_load(n_iter[0:1, 0:1], min_val=8, max_val=16)
            with pe.Fori(0, n) as it:
                for e in range(2):
                    for m in range(2):
                        bank = ps[4 + m][:, :]
                        if e == 0:
                            pe.wait_ge(xg_lo_ready, 4 * it + 4)
                        else:
                            pe.wait_ge(comb_ready, it + 1)
                        for q in range(4):
                            uq = 12 * e + 4 * m + q
                            pe.wait_ge(ex_hi_ready, 24 * it + uq + 1)
                            pe.wait_ge(ex_lo_ready, 24 * it + (uq + 1 + 12))
                            wh, wl = ex_hi[uq % 4], ex_lo[uq % 4]
                            for j in range(2):
                                k = 2 * q + j
                                xh, xlo = (x[:, k, e * P:(e + 1) * P] for x in (xg_hi, xg_lo))
                                pe.matmul(bank, xh, wh[:, j, :], start=k == 0, stop=False)
                                pe.matmul(bank, xlo, wh[:, j, :], start=False, stop=False)
                                mm = pe.matmul(bank, xh, wl[:, j, :], start=False, stop=k == KD - 1)
                            mm.then_inc(ex_done, 1)
                    scatter(1 - e, 4 * it + (2 * e + 2))
                    pe.wait_ge(hid_ready, 2 * it + (e + 1))
                    mm = transposes(ps[6], P, [hid[:, f * P:(f + 1) * P] for f in range(4)])
                    mm.then_inc(hid_tp, 1)
                    if e == 0:
                        mm = transposes(ps[7], P, [pick[:, b, x, :].bitcast(F32) for x in range(2) for b in range(TB)])
                        mm.then_inc(put_tp, 1)
                        for x in range(2):
                            for b in range(TB):
                                mm = pe.matmul(ps[4][:, x:x + 1], pick[:, b, x, :].bitcast(F32), combs[:, it, b, x:x + 1],
                                               start=b == 0, stop=b == 1)
                        mm.then_inc(comb_mm, 1)
                        pe.wait_ge(put_ready, it + 1)
                    else:
                        pe.wait_ge(pick_ready, it + 2)
                        gather(4 * it + 4)
                        pe.wait_ge(xg_lo_ready, 4 * it + 5)
                    pe.wait_ge(hid_hi_ready, 2 * it + (e + 1))
                    pe.wait_ge(hid_lo_ready, 2 * it + (e + 1))
                    for f in range(4):
                        uq = 12 * e + 8 + f
                        pe.wait_ge(ex_hi_ready, 24 * it + (uq + 1))
                        pe.wait_ge(ex_lo_ready, 24 * it + (uq + 1 + 12))
                        wh, wl = ex_hi[uq % 4], ex_lo[uq % 4]
                        for half in range(2):
                            bank = ps[6 + half][:, :]
                            pe.matmul(bank, hid_hi[:, f, :], wh[:, half, :], start=f == 0, stop=False)
                            pe.matmul(bank, hid_lo[:, f, :], wh[:, half, :], start=False, stop=False)
                            mm = pe.matmul(bank, hid_hi[:, f, :], wl[:, half, :], start=False, stop=f == 3)
                        mm.then_inc(ex_done, 1)
            pe.wait_ge(y_lo_ready, 4 * n + 2)
            for b in range(TB):
                for half in range(2):
                    for y in (y_hi, y_lo):
                        mm = pe.matmul(ps[2 * b + half][:, :], put[:, 1, b, :], y[:, half * 512:(half + 1) * 512],
                                       start=False, stop=y is y_lo, skip_group_check=True)
            mm.then_inc(moe_done, 1)

        @block.scalar
        def _(act):
            act.wait_ge(par_in, 16)
            act.activation(cond[:, :, :], par[:, C_COND:C_COND + 16].rearrange("p (k c) -> p k c", c=2), ACT.Silu)\
               .then_inc(cond_ready, 1)
            act.wait_ge(x_loaded, 16)
            act.activation(x_sq[:, :, :], x_in[:, :, :], ACT.Square).then_inc(sq_ready, 1)
            act.wait_ge(ms_read, 1)
            act.activation(rms_in[:, :], mean_sq[:, :], ACT.Sqrt).then_inc(rms_ready, 1)
            for j in range(4):
                act.wait_ge(ada_mm, j + 1)
                act.activation(mod_row[:, j * 512:(j + 1) * 512], ps[1 + j][0:2, :], ACT.Copy).then_inc(mod_row_ready, 1)
            for k in range(KD):
                act.wait_ge(u_f, 2 * k + 2)
                act.activation(u_hi[:, :, k, :], x_in[:, k, :].rearrange("p (a t) -> p a t", a=2), ACT.Copy)\
                   .then_inc(u_hi_ready, 1)

            def hi(u):
                act.wait_ge(raw_full[u % RAW], 16 * (u // RAW + 1))
                if u >= 2:
                    act.wait_ge(unit_done, u - 1)
                m = 64 if u == U_DT else P
                act.activation(w_hi[u % 2][:, :, 0:m], raw[:, u % RAW, :, 0:m], ACT.Copy).then_inc(split_hi, 1)

            def out_of_psum(u):
                if u < 0:
                    return
                bank = ps[u % 2]
                act.wait_ge(unit_done, u + 1)
                if u == U_DT:
                    act.wait_ge(headrow_in, 16)
                    act.activation(dt_e[:, :], bank[0:64, :], ACT.Abs, bias=headrow[:, 0:1]).then_inc(act_dt, 1)
                elif u < U_Z:
                    t = u - U_B
                    tile = t + 16 if u < U_X else t - 8
                    n = 2 if u < U_C or u >= U_X else 1
                    if t >= 2:
                        act.wait_ge(conv_done, t - 1)
                    act.activation(conv[t % 2][:, 0:n, :], bank[:, 0:n * T].rearrange("p (a t) -> p a t", a=n), ACT.Identity,
                                   bias=c_(C_CB + tile), scale=c_(C_CW + 4 * tile + 1)).then_inc(conv_init, 1)
                elif u < U_CH:
                    if u == U_Z:
                        act.wait_ge(ada_stored, 16)
                    act.activation(z[:, u - U_Z, :], bank[:, 0:T], ACT.Copy).then_inc(copied, 1)
                elif u < U_GATEB:
                    i = (u - U_CH) // 2
                    if (u - U_CH) % 2 == 0:
                        if i >= 2:
                            act.wait_ge(v_chain, 3 * (i - 1))
                        act.activation(v_tmp[i % 2][:, :], bank[:, 0:T], ACT.Copy).then_inc(copied, 1)
                elif U_MB <= u < U_MA:
                    act.activation(m_b[:, u - U_MB, :], bank[:, 0:T], ACT.Copy).then_inc(copied, 1)
                elif U_MA <= u < U_SC:
                    act.activation(m_a[:, u - U_MA, :], bank[:, 0:T], ACT.Copy).then_inc(copied, 1)

            def silu(t):
                u = t + U_B
                if t < 0 or u >= U_Z:
                    return
                act.wait_ge(conv_tap, 3 * t + 3)
                src = conv[t % 2]
                if u < U_C:
                    act.activation(bc[:, t, :], src[:, 0, :], ACT.Silu)
                    act.activation(bl[:, t, :], src[:, 1, :], ACT.Silu).then_inc(conv_done, 1)
                elif u < U_X:
                    act.activation(cl[:, u - U_C, :], src[:, 0, :], ACT.Silu).then_inc(conv_done, 1)
                else:
                    act.activation(xc[:, u - U_X, :], src[:, 0, :], ACT.Silu)
                    act.activation(xl[:, u - U_X, :], src[:, 1, :], ACT.Silu).then_inc(conv_done, 1)

            def gate_hi(i):
                act.wait_ge(gated, i + 1)
                act.activation(gb_hi[:, i, :], gb_tmp[i % 2][:, :], ACT.Copy).then_inc(gb_hi_ready, 1)

            def piece_out(n):
                if n is None:
                    return
                kind, g = PIECES[n]
                if kind not in BY_ACT:
                    return
                act.wait_ge(piece, n + 1)
                if kind == "tables":
                    act.activation(tok[:, :, :, :], ps[6][:, :].rearrange("p (b k h) -> p b k h", b=2, k=4), ACT.Copy)\
                       .then_inc(piece_act, 1)
                elif kind == "b_ctx":
                    act.activation(b_tok[:, 0:4, :], ps[6][:, :].rearrange("p (b k) -> p b k", b=4), ACT.Copy)
                    act.activation(b_tok[:, 4:8, :], ps[7][:, :].rearrange("p (b k) -> p b k", b=4), ACT.Copy)\
                       .then_inc(piece_act, 1)
                elif kind == "state":
                    act.activation(state[:, g, 0, :], ps[6][:, :], ACT.Copy)
                    act.activation(state[:, g, 1, :], ps[7][:, :], ACT.Copy).then_inc(piece_act, 1)
                elif kind == "x_lat":
                    act.activation(xn[g % 2][:, 0, :], ps[6][:, :], ACT.Copy)
                    act.activation(xn[g % 2][:, 1, :], ps[7][:, :], ACT.Copy).then_inc(piece_act, 1)
                else:
                    act.wait_ge(piece_dve, dve_pieces(n + 1))
                    act.activation(cb_off[g % 2][:, :, :], ps[7][:, :].rearrange("p (s k l) -> p s k l", s=2, k=2)[:, :, 1, :],
                                   ACT.Copy).then_inc(piece_act, 1)

            for u in range(U_CH):
                hi(u)
                out_of_psum(u - 2)
                silu(u - 3 - U_B)
                if u == 3:
                    act.wait_ge(act_dt, 1)
                    act.activation(dt_e[:, :], dt_e[:, :], ACT.Exp, scale=-1.0).then_inc(act_dt, 1)
                    act.activation(a_pos[:, :], headrow[:, 1:2], ACT.Exp).then_inc(act_dt, 1)
                if u == 16:
                    act.wait_ge(dve_dt, DT_REV)
                    act.activation(w_ctx[0:32, 0, :], rev[0:32, 0, :], ACT.Exp, bias=cum[0:32, 1, P - 1:P])
                    act.activation(w_ctx[0:32, 1, :], rev[0:32, 1, :], ACT.Exp).then_inc(act_dt, 1)
                    act.activation(w_ctx[32:64, 1, :], rev[32:64, 1, :], ACT.Exp, bias=cum[32:64, 0, 0:1])
                    act.activation(w_ctx[32:64, 0, :], rev[32:64, 0, :], ACT.Exp).then_inc(act_dt, 1)
                    act.activation(dec_t[0:32, 0, :], cum[0:32, 2, :], ACT.Exp)
                    act.activation(dec_t[0:32, 1, :], cum[0:32, 3, :], ACT.Exp, bias=cum[0:32, 2, P - 1:P]).then_inc(act_dt, 1)
                    act.activation(dec_t[32:64, 1, :], cum[32:64, 3, :], ACT.Exp).then_inc(act_dt, 1)
                    act.activation(dec_t[32:64, 0, :], cum[32:64, 2, :], ACT.Exp, bias=cum[32:64, 3, 0:1]).then_inc(act_dt, 1)
                piece_out(piece_at_unit(u - 1))

            def decays(h):
                e = dec[h % 2]
                act.wait_ge(expo_ready, h + 1)
                if h >= 2:
                    act.wait_ge(mix_ready, h - 1)
                rows = ps[2 + h % 2]
                act.activation(e[:, 0:2, :], expo[:, :, :], ACT.Exp)
                act.activation(e[:, 2, :], rows[:, P:2 * P], ACT.Exp, bias=tok[:, 0, 2, h:h + 1])
                act.activation(e[:, 3, :], rows[:, T:T + P], ACT.Exp, bias=tok[:, 1, 2, 32 + h:33 + h]).then_inc(dec_ready, 1)

            for s in range(HEADS + 5):
                for u in range(first_unit_of_step(s), first_unit_of_step(s + 1)):
                    hi(u)
                    out_of_psum(u - 2)
                    if U_GATEB + 3 <= u < U_MB + 3:
                        gate_hi(u - 3 - U_GATEB)
                piece_out(piece_at_unit(U_CH - 1) if s == 0 else piece_at_step(s - 1))
                if s < HEADS:
                    decays(s)
            for u in (U_SC, U_SC + 1):
                hi(u)
                out_of_psum(u - 2)
            act.wait_ge(copied, 40)
            act.activation(m_b[:, :, :], m_b[:, :, :], ACT.Sigmoid).then_inc(sig_ready, 1)
            act.activation(m_a[:, :, :], m_a[:, :, :], ACT.Sigmoid).then_inc(sig_ready, 1)
            hi(U_SC + 2)
            for i in range(4):
                act.activation(z[:, 4 * i:4 * i + 4, :], z[:, 4 * i:4 * i + 4, :], ACT.Silu).then_inc(z_act, 1)
            for i in range(4):
                hi(U_SC + 3 + i)
                act.wait_ge(gy_made, i + 1)
                for t in range(4 * i, 4 * i + 4):
                    act.activation(gg_hi[:, t, :], xl[:, t, :], ACT.Copy, scale=c_(C_SSDN + t)).then_inc(gg_hi_ready, 1)
            hi(U_SSD - 1)
            hi(U_SSD)
            act.wait_ge(ms2_ready, 1)
            act.activation(rms2[:, :], rms2[:, :], ACT.Sqrt).then_inc(rms2_ready, 1)
            for u in range(U_SSD + 1, U_END):
                hi(u)
                if u >= U_SSD + 4 and (u - U_SSD) % 2 == 0 and (u - U_SSD - 4) // 2 < KD:
                    n = (u - U_SSD - 4) // 2
                    act.wait_ge(merge_made, n + 1)
                    act.activation(m_hi[:, n, :], merged[n % 2][:, :], ACT.Copy).then_inc(m_hi_ready, 1)
            for b in range(TB):
                act.wait_ge(h_chain, 4 * b + 4)
                act.activation(u2[:, b, :], h[:, b, :], ACT.Square, accum_out=stat[:, b:b + 1]).then_inc(h_sq, 1)
            act.wait_ge(h_ms, 1)
            act.activation(stat[:, 2:4], stat[:, 2:4], ACT.Sqrt).then_inc(h_rms, 1)
            for b in range(TB):
                act.wait_ge(u2_chain, 2 * b + 2)
                act.activation(u2_hi[:, b, :], u2[:, b, :], ACT.Copy).then_inc(u2_hi_ready, 1)
            act.wait_ge(u2_tp, 1)
            for i in range(2):
                op = act.activation(u2_t[:, 2 * i:2 * i + 2, :], ps[i][:, :].rearrange("p (k t) -> p k t", k=2), ACT.Copy)
            op.then_inc(u2_t_act, 1)
            act.wait_ge(logits_done, 1)
            act.activation(score[:, :, :], ps[2][:, 0:2 * NE].rearrange("p (b e) -> p b e", b=TB), ACT.Sigmoid)\
               .then_inc(score_ready, 1)

            def ex_split(it, q):
                act.wait_ge(ex_full[q % 12 // 4], 32 * it + 16 * (q // 12 + 1))
                act.wait_ge(ex_done, 24 * it + (q + 1))
                r = q % 4
                act.activation(ex_hi[r][:, :, :], ex_raw[q % 12 // 4][:, 2 * r:2 * r + 2, :], ACT.Copy).then_inc(ex_hi_ready, 1)

            def y_out(e, done, index):
                act.wait_ge(ex_done, done)
                act.wait_ge(scattered, index + 1)
                for half in range(2):
                    act.activation(y_hi[:, half * 512:(half + 1) * 512], ps[6 + half][:, :], ACT.Copy,
                                   scale=comb_slot[:, e:e + 1]).then_inc(y_hi_ready, 1)

            def gather_out(first):
                for r in range(4):
                    act.wait_ge(gathered, first + (r + 1))
                    act.activation(xg_hi[:, 2 * r:2 * r + 2, :], ps[(7, 4, 5, 4)[r]][:, :].rearrange("p (k t) -> p k t", k=2),
                                   ACT.Copy).then_inc(xg_hi_ready, 1)

            gather_out(0)
            act.wait_ge(route, ROUTE_N)
            n = act.value_load(n_iter[0:1, 0:1], min_val=8, max_val=16)
            with act.Fori(0, n) as it:
                for q in range(3):
                    ex_split(it, q)
                act.wait_ge(zeros_made, 3)
                act.wait_ge(xg_lo_ready, 4 * it + 4)
                y_out(1, 24 * it + 4, 2 * it)
                for e in range(2):
                    for q in range(3, 9):
                        ex_split(it, 12 * e + q)
                    act.wait_ge(ex_done, 24 * it + (12 * e + 8))
                    act.activation(act_g[:, :], ps[4][:, :], ACT.Silu).then_inc(act_g_ready, 1)
                    for q in range(9, 12):
                        ex_split(it, 12 * e + q)
                    act.wait_ge(hid_tp, 2 * it + (e + 1))
                    act.activation(hid_hi[:, :, :], ps[6][:, :].rearrange("p (f t) -> p f t", f=4), ACT.Copy)\
                       .then_inc(hid_hi_ready, 1)
                    if e == 0:
                        act.wait_ge(put_tp, it + 1)
                        act.activation(put[:, :, :, :], ps[7][:, :].rearrange("p (x b t) -> p x b t", x=2, b=TB), ACT.Copy)\
                           .then_inc(put_ready, 1)
                        for q in range(12, 15):
                            ex_split(it, q)
                        act.wait_ge(comb_ready, it + 1)
                        y_out(0, 24 * it + 16, 2 * it + 1)
                    else:
                        gather_out(4 * it + 4)
            y_out(1, 24 * n + 4, 2 * n)
            for b in range(TB):
                act.wait_ge(fin, 4 * b + 4)
                act.activation(x_nat[:, b, :], result[:, b, :], ACT.Square, accum_out=stat[:, b:b + 1]).then_inc(fin_sq, 1)
            act.wait_ge(fin, FIN_OUT - 2)
            act.activation(stat[:, 2:4], stat[:, 2:4], ACT.Sqrt).then_inc(fin_rms, 1)

        @block.vector
        def _(dve):
            dve.sem_inc(ex_lo_ready, 12)
            dve.wait_ge(par_in, 16)
            dve.wait_ge(ms_done, 1)
            dve.tensor_scalar(mean_sq[:, :], ps[0][:, :], 1.0 / D, EPS, ALU.mult, ALU.add).then_inc(ms_read, 1)
            dve.wait_ge(rms_ready, 1)
            dve.reciprocal(rstd_in[:, :], rms_in[:, :]).then_inc(xn_chain, 1)
            dve.wait_ge(x_loaded, 16)
            dve.wait_ge(sq_ready, 1)
            dve.wait_ge(xn_chain, 1)
            dve.tensor_tensor(x_in[:, :, :], x_in[:, :, :], rstd_in[:, :].unsqueeze(1).to_broadcast([P, KD, 2 * T]), ALU.mult)\
               .then_inc(xn_chain, 1)
            dve.wait_ge(cond_ready, 1)
            dve.tensor_copy(cond_keep[:, :], cond[:, :, 0]).then_inc(xn_chain, 1)
            dve.wait_ge(mod_tp, 1)
            dve.tensor_tensor(mod_col[:, :, :], ps[5][:, 0:32].rearrange("p (t c) -> p t c", c=2),
                              par[:, C_BADA:C_BADA + 16].unsqueeze(2).to_broadcast([P, 16, 2]), ALU.add).then_inc(mod_ready, 1)
            dve.wait_ge(mod_ready, 1)
            dve.scalar_tensor_tensor(gain_col[:, :, :], mod_col[:, 8:16, :], 1.0,
                                     par[:, C_NMIX:C_NMIX + 8].unsqueeze(2).to_broadcast([P, 8, 2]), ALU.add, ALU.mult)\
               .then_inc(mod_ready, 1)
            dve.wait_ge(mod_ready, 2)
            dve.wait_ge(xn_chain, 2)
            for k in range(KD):
                for half in range(2):
                    c = 1 - half
                    v = x_in[:, k, half * T:(half + 1) * T]
                    dve.tensor_scalar(v, v, gain_col[:, k, c:c + 1], mod_col[:, k, c:c + 1], ALU.mult, ALU.add)\
                       .then_inc(u_f, 1)
            for k in range(KD):
                dve.wait_ge(u_hi_ready, k + 1)
                dve.tensor_tensor(u_lo[:, :, k, :], x_in[:, k, :].rearrange("p (a t) -> p a t", a=2),
                                  u_hi[:, :, k, :].bitcast(F32), ALU.subtract).then_inc(u_lo_ready, 1)

            def lo(u):
                dve.wait_ge(split_hi, u + 1)
                if u >= 2:
                    dve.wait_ge(unit_done, u - 1)
                m = 64 if u == U_DT else P
                dve.tensor_tensor(w_lo[u % 2][:, :, 0:m], raw[:, u % RAW, :, 0:m], w_hi[u % 2][:, :, 0:m].bitcast(F32),
                                  ALU.subtract).then_inc(split_lo, 1)

            def out_of_psum(u):
                if u < 0:
                    return
                bank = ps[u % 2]
                if u == U_DT:
                    dve.wait_ge(act_dt, 1)
                    dve.tensor_scalar(dt_r[:, :], bank[0:64, :], headrow[:, 0:1], 0.0, ALU.add, ALU.max).then_inc(dt_read, 1)
                elif u < U_Z:
                    t = u - U_B
                    tile = t + 16 if u < U_X else t - 8
                    n = 2 if u < U_C or u >= U_X else 1
                    dve.wait_ge(conv_init, t + 1)
                    src = bank[:, 0:n * T].rearrange("p (a t) -> p a t", a=n)
                    acc = conv[t % 2][:, 0:n, :]
                    for i, (tap, o, s, w) in enumerate(((0, 1, 0, T - 1), (2, 0, 1, T - 1), (3, 0, 2, T - 2))):
                        if i:
                            dve.wait_ge(conv_tap, 3 * t + i)
                        op = dve.scalar_tensor_tensor(acc[:, :, o:o + w], src[:, :, s:s + w], c_(C_CW + 4 * tile + tap),
                                                      acc[:, :, o:o + w], ALU.mult, ALU.add)
                        op.then_inc(conv_tap, 1)
                elif U_CH <= u < U_GATEB and (u - U_CH) % 2 == 1:
                    i = (u - U_CH) // 2
                    v = v_tmp[i % 2]
                    dve.wait_ge(unit_done, u + 1)
                    dve.wait_ge(copied, 16 + i + 1)
                    dve.tensor_tensor(v[:, :], v[:, :], bank[:, 0:T], ALU.mult).then_inc(v_made, 1)
                    dve.wait_ge(v_made, i + 1)
                    vg = v[:, :].rearrange("p (r w) -> p r w", w=64)
                    og = vc[:, i, :].rearrange("p (r w) -> p r w", w=64)
                    dve.tensor_scalar(vc[:, i, :], v[:, :], c_(C_SCW + 3 * i + 1), None, ALU.mult).then_inc(v_chain, 1)
                    dve.wait_ge(v_chain, 3 * i + 1)
                    dve.scalar_tensor_tensor(og[:, :, 1:64], vg[:, :, 0:63], c_(C_SCW + 3 * i), og[:, :, 1:64],
                                             ALU.mult, ALU.add).then_inc(v_chain, 1)
                    dve.wait_ge(v_chain, 3 * i + 2)
                    dve.scalar_tensor_tensor(og[:, :, 0:63], vg[:, :, 1:64], c_(C_SCW + 3 * i + 2), og[:, :, 0:63],
                                             ALU.mult, ALU.add).then_inc(v_chain, 1)
                elif U_GATEB <= u < U_MB:
                    i = u - U_GATEB
                    dve.wait_ge(unit_done, u + 1)
                    if i >= 2:
                        dve.wait_ge(gb_lo_ready, i - 1)
                    dve.wait_ge(v_chain, 3 * i + 3)
                    dve.tensor_tensor(gb_tmp[i % 2][:, :], vc[:, i, :], bank[:, 0:T], ALU.mult).then_inc(gated, 1)

            def gate_lo(i):
                dve.wait_ge(gb_hi_ready, i + 1)
                dve.tensor_tensor(gb_lo[:, i, :], gb_tmp[i % 2][:, :], gb_hi[:, i, :].bitcast(F32), ALU.subtract)\
                   .then_inc(gb_lo_ready, 1)

            def softplus(step):
                n = [0]

                def chain(op):
                    op.then_inc(dve_dt, 1)
                    n[0] += 1
                    dve.wait_ge(dve_dt, DT_AT[step] + n[0])

                if step == 0:
                    dve.wait_ge(act_dt, 3)
                    chain(dve.tensor_scalar(dt_t[:, :], dt_e[:, :], 2.0, None, ALU.add))
                    chain(dve.reciprocal(dt_t[:, :], dt_t[:, :]))
                    chain(dve.tensor_tensor(dt_t[:, :], dt_t[:, :], dt_e[:, :], ALU.mult))
                    chain(dve.tensor_tensor(dt_t2[:, :], dt_t[:, :], dt_t[:, :], ALU.mult))
                elif step == 1:
                    chain(dve.tensor_scalar(dt_q[:, :], dt_t2[:, :], LOG1P[7], None, ALU.mult))
                    for j in (6, 5, 4):
                        chain(dve.scalar_tensor_tensor(dt_q[:, :], dt_q[:, :], LOG1P[j], dt_t2[:, :], ALU.add, ALU.mult))
                elif step == 2:
                    for j in (3, 2, 1):
                        chain(dve.scalar_tensor_tensor(dt_q[:, :], dt_q[:, :], LOG1P[j], dt_t2[:, :], ALU.add, ALU.mult))
                    chain(dve.scalar_tensor_tensor(dt_q[:, :], dt_q[:, :], 1.0, dt_t[:, :], ALU.add, ALU.mult))
                elif step == 3:
                    dve.wait_ge(dt_read, 1)
                    flat = dt[:, :, :].rearrange("p c l -> p (c l)")
                    chain(dve.scalar_tensor_tensor(flat, dt_q[:, :], 2.0, dt_r[:, :], ALU.mult, ALU.add))
                    chain(dve.tensor_scalar(dt_q[:, :], flat, a_pos[:, 0:1], -1.0, ALU.mult, ALU.mult))
                elif step in (4, 5):
                    d = step - 4
                    r = slice(32 * d, 32 * d + 32)
                    q = dt_q[:, :].rearrange("p (c l) -> p c l", l=P)
                    way = slice(None) if d == 0 else slice(None, None, -1)
                    for c in range(4):
                        chain(dve.tensor_tensor_scan(cum[r, c, way], q[r, c, way], q[r, c, way], 0.0, ALU.add, ALU.bypass))
                elif step == 6:
                    for d in range(2):
                        r = slice(32 * d, 32 * d + 32)
                        end = P - 1 if d == 0 else 0
                        for c in range(4):
                            chain(dve.tensor_scalar(rev[r, c, :], cum[r, c, :], cum[r, c, end:end + 1], -1.0,
                                                    ALU.subtract, ALU.mult))
                else:
                    dve.wait_ge(act_dt, 8)
                    chain(dve.tensor_tensor(coef_t[:, :, :], w_ctx[:, :, :], dt[:, 0:2, :], ALU.mult))

            def ada_chunk(j):
                dve.wait_ge(wa_full[j % 2], 16 * ((j + 4) // 2 + 1))
                for k in range(KD):
                    n = 8 * j + k
                    src = wa[j % 2][:, k, :]
                    if k == 0:
                        op = dve.tensor_scalar(ada_sum[:, j, :], src, cond_keep[:, 0:1], None, ALU.mult)
                    else:
                        dve.wait_ge(ada_acc, n)
                        op = dve.scalar_tensor_tensor(ada_sum[:, j, :], src, cond_keep[:, k:k + 1], ada_sum[:, j, :],
                                                      ALU.mult, ALU.add)
                    op.then_inc(ada_acc, 1)

            def ada_out(j):
                dve.wait_ge(ada_summed, j + 1)
                if j == 0:
                    dve.wait_ge(b_row_in, 16)
                dve.tensor_tensor(ada_row[:, j * 512:(j + 1) * 512], ps[2 + j % 2][0:1, :], b_row[:, j * 512:(j + 1) * 512],
                                  ALU.add).then_inc(ada_row_ready, 1)

            def piece_out(n):
                if n is None:
                    return
                kind, g = PIECES[n]
                if kind not in BY_DVE:
                    return
                dve.wait_ge(piece, n + 1)
                if kind == "tables":
                    dve.tensor_copy(coef[:, :, :], ps[7][:, 0:P].rearrange("p (b h) -> p b h", b=2)).then_inc(piece_dve, 1)
                elif kind == "x_ctx":
                    for b in range(2):
                        for d in range(2):
                            op = dve.tensor_tensor(
                                xw[:, b, d, :].rearrange("p (h w) -> p h w", w=64), ps[6 + b][:, :].rearrange("p (h w) -> p h w", w=64),
                                coef[:, b, 32 * d + 8 * g:32 * d + 8 * g + 8].unsqueeze(2).to_broadcast([P, 8, 64]), ALU.mult)
                    op.then_inc(piece_dve, 1)
                elif kind == "cb":
                    diag = ps[7][:, :].rearrange("p (s k l) -> p s k l", s=2, k=2)[:, :, 0, :]
                    dve.tensor_tensor(cb_up[g % 2][:, :, :], diag, c_(C_UP, P).unsqueeze(1).to_broadcast([P, 2, P]), ALU.mult)
                    dve.tensor_tensor(cb_lo[g % 2][:, :, :], diag, c_(C_LO, P).unsqueeze(1).to_broadcast([P, 2, P]), ALU.mult)\
                       .then_inc(piece_dve, 1)
                else:
                    gg, l = g // 2, g % 2
                    y = yi[gg % 2][:, l, :]
                    n_c = 2 * (2 * gg + l)

                    def by(d):
                        return tok[:, l, 3, 32 * d + 8 * gg:32 * d + 8 * gg + 8].unsqueeze(2).to_broadcast([P, 8, 64])

                    def heads(ap):
                        return ap.rearrange("p (h w) -> p h w", w=64)

                    dve.tensor_tensor(heads(y), heads(ps[6][:, :]), by(0), ALU.mult).then_inc(carry_chain, 1)
                    dve.tensor_tensor(heads(yi_tmp[:, :]), heads(ps[7][:, :]), by(1), ALU.mult).then_inc(carry_chain, 1)
                    dve.wait_ge(carry_chain, n_c + 2)
                    dve.tensor_tensor(y, y, yi_tmp[:, :], ALU.add).then_inc(piece_dve, 1)

            for u in range(U_CH):
                lo(u)
                out_of_psum(u - 2)
                if 4 <= u < 11:
                    softplus(u - 4)
                if u == 17:
                    softplus(7)
                if u >= 4 and (u - 4) % 2 == 0 and (u - 4) // 2 < 8:
                    ada_chunk((u - 4) // 2)
                if u == U_Z:
                    for j in range(8):
                        ada_out(j)
                piece_out(piece_at_unit(u - 1))

            def exponents(h):
                g = h // 8
                rows = ps[2 + h % 2]
                dve.wait_ge(rows_done, h + 1)
                if h >= 1:
                    dve.wait_ge(dec_ready, h)
                    dve.wait_ge(wd_ready, 2 * h)
                for b in range(2):
                    dve.tensor_scalar(back[:, b, :], rows[:, T + b * P:T + (b + 1) * P], tok[:, b, 0, 32 + h:33 + h], None,
                                      ALU.subtract).then_inc(scan_chain, 1)
                for b in range(2):
                    dve.tensor_scalar(wd_tmp[:, b, :], cb_lo[g % 2][:, b, :], tok[:, b, 1, 32 + h:33 + h], None,
                                      ALU.mult).then_inc(scan_chain, 1)
                dve.wait_ge(scan_chain, 4 * h + 2)
                for b in range(2):
                    op = dve.scalar_tensor_tensor(expo[:, b, :], rows[:, b * P:(b + 1) * P], tok[:, b, 0, h:h + 1],
                                                  back[:, b, :], ALU.subtract, ALU.min)
                op.then_inc(expo_ready, 1)
                dve.wait_ge(scan_chain, 4 * h + 4)
                for b in range(2):
                    dve.scalar_tensor_tensor(wd[h % 2][:, b, :], cb_up[g % 2][:, b, :], tok[:, b, 1, h:h + 1],
                                             wd_tmp[:, b, :], ALU.mult, ALU.add).then_inc(wd_ready, 1)

            def mixing(h):
                g = h // 8
                e, m = dec[h % 2], mix[h % 2]
                dve.wait_ge(dec_ready, h + 1)
                dve.wait_ge(wd_ready, 2 * h + 2)
                if h >= 2:
                    dve.wait_ge(y_done, h - 1)
                for b in range(2):
                    dve.tensor_tensor(m[:, 3 * b, :], e[:, b, :], wd[h % 2][:, b, :], ALU.mult)
                for b in range(2):
                    op = dve.scalar_tensor_tensor(m[:, 1 + b, :], e[:, 2 + b, :], tok[:, b, 1, 32 * b + h:32 * b + h + 1],
                                                  cb_off[g % 2][:, b, :], ALU.mult, ALU.mult)
                op.then_inc(mix_ready, 1)

            def store_y(pair):
                dve.wait_ge(y_done, 2 * pair + 2)
                dve.scalar_tensor_tensor(xl[:, pair, :], xl[:, pair, :], c_(C_DSKIP + pair), ps[4 + pair % 2][:, 0:T],
                                         ALU.mult, ALU.add).then_inc(y_stored, 1)

            for s in range(HEADS + 5):
                for u in range(first_unit_of_step(s), first_unit_of_step(s + 1)):
                    lo(u)
                    out_of_psum(u - 2)
                    if U_GATEB + 3 <= u < U_MB + 3:
                        gate_lo(u - 3 - U_GATEB)
                piece_out(piece_at_unit(U_CH - 1) if s == 0 else piece_at_step(s - 1))
                if s < HEADS:
                    exponents(s)
                if 1 <= s <= HEADS:
                    mixing(s - 1)
                if s >= 4 and s % 2 == 0 and (s - 4) // 2 < 16:
                    store_y((s - 4) // 2)

            def branch(n):
                dve.wait_ge(unit_done, U_SC + n + 1)
                if n == 0:
                    dve.wait_ge(sig_ready, 1)
                dve.tensor_tensor(m_b[:, n, :], ps[(U_SC + n) % 2][:, 0:T], m_b[:, n, :], ALU.mult).then_inc(branch_b, 1)

            for n in range(3):
                lo(U_SC + n)
            branch(0)
            dve.wait_ge(y_stored, 16)
            for i in range(4):
                dve.wait_ge(z_act, i + 1)
                r = slice(4 * i, 4 * i + 4)
                dve.tensor_tensor(xl[:, r, :], xl[:, r, :], z[:, r, :], ALU.mult).then_inc(gy_made, 1)
                lo(U_SC + 3 + i)
                branch(1 + i)
                for t in range(4 * i, 4 * i + 4):
                    dve.wait_ge(gg_hi_ready, t + 1)
                    dve.scalar_tensor_tensor(gg_lo[:, t, :], xl[:, t, :], c_(C_SSDN + t), gg_hi[:, t, :].bitcast(F32),
                                             ALU.mult, ALU.subtract).then_inc(gg_lo_ready, 1)
            lo(U_SSD - 1)
            branch(5)
            lo(U_SSD)
            branch(6)
            branch(7)
            dve.wait_ge(ssq_done, 1)
            dve.tensor_scalar(rms2[:, :], ps[6][:, 0:T], 1.0 / INNER, EPS, ALU.mult, ALU.add).then_inc(ms2_ready, 1)
            dve.wait_ge(rms2_ready, 1)
            dve.reciprocal(rstd2[:, :], rms2[:, :]).then_inc(ma_scaled, 1)
            dve.wait_ge(sig_ready, 2)
            dve.wait_ge(ma_scaled, 1)
            dve.tensor_tensor(m_a[:, :, :], m_a[:, :, :], rstd2[:, :].unsqueeze(1).to_broadcast([P, KD, T]), ALU.mult)\
               .then_inc(ma_scaled, 1)

            def merge(n):
                dve.wait_ge(unit_done, U_SSD + 2 * n + 2)
                if n == 0:
                    dve.wait_ge(ma_scaled, 2)
                    dve.wait_ge(branch_b, KD)
                if n >= 2:
                    dve.wait_ge(m_lo_ready, n - 1)
                m = merged[n % 2][:, :]
                dve.tensor_tensor(m, ps[n % 2][:, 0:T], m_a[:, n, :], ALU.mult).then_inc(merge_chain, 1)
                dve.wait_ge(merge_chain, n + 1)
                dve.tensor_tensor(m, m, m_b[:, n, :], ALU.add).then_inc(merge_made, 1)

            def merge_lo(n):
                dve.wait_ge(m_hi_ready, n + 1)
                dve.tensor_tensor(m_lo[:, n, :], merged[n % 2][:, :], m_hi[:, n, :].bitcast(F32), ALU.subtract)\
                   .then_inc(m_lo_ready, 1)

            for u in range(U_SSD + 1, U_END):
                lo(u)
                n, odd = (u - U_SSD - 2) // 2, (u - U_SSD) % 2
                if n >= 0 and odd and n < KD:
                    merge(n)
                if n >= 1 and not odd and n <= KD:
                    merge_lo(n - 1)
            dve.wait_ge(norm_rows_in, 16)
            dve.wait_ge(mod_rest_in, 16)
            dve.scalar_tensor_tensor(norm_rows[:, 0, :], mod_rest[:, 2, :], 1.0, norm_rows[:, 0, :], ALU.add, ALU.mult)\
               .then_inc(nf_made, 1)
            dve.wait_ge(unit_done, U_END)
            dve.wait_ge(x_nat_in, 16)

            def halves(half):
                return slice(half * 512, (half + 1) * 512)

            for b in range(TB):
                for half in range(2):
                    dve.tensor_tensor(h[:, b, halves(half)], ps[2 + 2 * b + half][:, :], mod_rest[:, 0, halves(half)],
                                      ALU.mult).then_inc(h_chain, 1)
                for half in range(2):
                    dve.wait_ge(h_chain, 4 * b + half + 1)
                    dve.tensor_tensor(h[:, b, halves(half)], h[:, b, halves(half)], x_nat[:, b, halves(half)],
                                      ALU.add).then_inc(h_chain, 1)
            dve.wait_ge(h_sq, TB)
            dve.tensor_scalar(stat[:, 2:4], stat[:, 0:2], 1.0 / D, EPS, ALU.mult, ALU.add).then_inc(h_ms, 1)
            dve.wait_ge(h_rms, 1)
            dve.reciprocal(stat[:, 2:4], stat[:, 2:4]).then_inc(h_ms, 1)
            dve.wait_ge(h_ms, 2)
            dve.wait_ge(nf_made, 1)
            for b in range(TB):
                dve.scalar_tensor_tensor(u2[:, b, :], h[:, b, :], stat[:, 2 + b:3 + b], norm_rows[:, 0, :], ALU.mult, ALU.mult)\
                   .then_inc(u2_chain, 1)
                dve.wait_ge(u2_chain, 2 * b + 1)
                dve.tensor_tensor(u2[:, b, :], u2[:, b, :], mod_rest[:, 1, :], ALU.add).then_inc(u2_chain, 1)
            dve.wait_ge(u2_tp, 1)
            for i in range(2):
                op = dve.tensor_copy(u2_t[:, 4 + 2 * i:6 + 2 * i, :], ps[6 + i][:, :].rearrange("p (k t) -> p k t", k=2))
            op.then_inc(u2_t_dve, 1)
            dve.wait_ge(h_chain, 4 * TB)
            dve.memset(zero_r[:, :].bitcast(F32), 0.0).then_inc(zeros_made, 1)
            dve.memset(put[:, :, :, :].bitcast(F32), 0.0).then_inc(zeros_made, 1)
            dve.memset(comb_slot[:, :], 0.0).then_inc(zeros_made, 1)
            for b in range(TB):
                dve.wait_ge(u2_hi_ready, b + 1)
                dve.tensor_tensor(u2_lo[:, b, :], u2[:, b, :], u2_hi[:, b, :].bitcast(F32), ALU.subtract).then_inc(u2_lo_ready, 1)

            n_route = [0]

            def step(op):
                op.then_inc(route, 1)
                n_route[0] += 1
                dve.wait_ge(route, n_route[0])

            def ranks(values, n, to):
                v_j = values.unsqueeze(2).to_broadcast([P, n, 4, 4])
                v_i = values.unsqueeze(3).to_broadcast([P, n, 4, 4])
                gt, ge = cmp_gt[:, 0:n], cmp_ge[:, 0:n]

                def mask(m, c):
                    f = m.rearrange("p c i j -> p c (i j)")
                    step(dve.tensor_tensor(f, f, c_(c, 16).unsqueeze(1).to_broadcast([P, n, 16]), ALU.mult))

                step(dve.tensor_tensor(gt, v_j, v_i, ALU.is_gt))
                step(dve.tensor_tensor(ge, v_j, v_i, ALU.is_ge))
                mask(gt, C_NTRI)
                mask(ge, C_TRI)
                step(dve.tensor_tensor(gt, gt, ge, ALU.add))
                step(dve.tensor_reduce(to, gt, AX_X, ALU.add))

            def by4(ap):
                return ap.rearrange("p b (g e) -> p (b g) e", e=4)

            dve.wait_ge(score_ready, 1)
            dve.wait_ge(b_rt_in, 16)
            step(dve.tensor_tensor(sel[:, :, :], score[:, :, :], b_rt[:, :].unsqueeze(1).to_broadcast([P, TB, NE]), ALU.add))
            ranks(by4(sel[:, :, :]), 8, rank[:, :, :])
            step(dve.tensor_scalar(top2[:, :, :], rank[:, :, :], 1.5, None, ALU.is_lt))
            step(dve.tensor_tensor(sel_top[:, :, :], top2[:, :, :], by4(sel[:, :, :]), ALU.mult))
            step(dve.tensor_reduce(g_score[:, :], sel_top[:, :, :], AX_X, ALU.add))
            ranks(g_score[:, :].rearrange("p (b g) -> p b g", b=TB), TB, g_rank[:, :].rearrange("p (b g) -> p b g", b=TB))
            step(dve.tensor_scalar(g_rank[:, :], g_rank[:, :], 0.5, None, ALU.is_lt))
            step(dve.tensor_tensor(by4(chosen[:, :, :]), top2[:, :, :], g_rank[:, :].unsqueeze(2).to_broadcast([P, 8, 4]),
                                   ALU.mult))
            assert n_route[0] == ROUTE_CHOSEN
            step(dve.tensor_tensor(comb[:, :, :], score[:, :, :], chosen[:, :, :], ALU.mult))
            step(dve.tensor_reduce(stat[:, 4:6], comb[:, :, :], AX_X, ALU.add))
            step(dve.reciprocal(stat[:, 4:6], stat[:, 4:6]))
            step(dve.tensor_tensor(comb[:, :, :], comb[:, :, :], stat[:, 4:6].unsqueeze(2).to_broadcast([P, TB, NE]), ALU.mult))

            def pairs(ap):
                return ap.rearrange("p b (i x) -> p i b x", x=2)

            for k in range(2):
                step(dve.tensor_copy(combs[:, 8 * k:8 * k + 8, :, :], pairs(comb[:, :, :])))
            dve.wait_ge(positions, 1)
            step(dve.tensor_tensor(slot[:, :, :], ps[3][:, 0:2 * NE].rearrange("p (b e) -> p b e", b=TB), chosen[:, :, :], ALU.mult))
            for k in range(2):
                step(dve.tensor_scalar(slots[:, 8 * k:8 * k + 8, :, :], pairs(slot[:, :, :]), -1.0 - P * k, None, ALU.add))
            assert n_route[0] == ROUTE_SLOTS
            step(dve.memset(slots[:, 16, :, :], -1.0))
            step(dve.tensor_reduce(stat[0:1, 6:7], ps[3][0:1, 2 * NE:3 * NE], AX_X, ALU.max))
            step(dve.tensor_scalar(stat[0:1, 6:7], stat[0:1, 6:7], float(P), 8.0, ALU.is_gt, ALU.mult))
            step(dve.tensor_scalar(n_iter[:, 0:1], stat[0:1, 6:7], 8.0, None, ALU.add))
            assert n_route[0] == ROUTE_N

            def ex_lo_(it, q):
                r = q % 4
                dve.wait_ge(ex_hi_ready, 24 * it + (q + 1))
                dve.tensor_tensor(ex_lo[r][:, :, :], ex_raw[q % 12 // 4][:, 2 * r:2 * r + 2, :], ex_hi[r][:, :, :].bitcast(F32),
                                  ALU.subtract).then_inc(ex_lo_ready, 1)

            def y_rest(e, index):
                for half in range(2):
                    dve.wait_ge(y_hi_ready, 2 * index + (half + 1))
                    dve.scalar_tensor_tensor(y_lo[:, halves(half)], ps[6 + half][:, :], comb_slot[:, e:e + 1],
                                             y_hi[:, halves(half)].bitcast(F32), ALU.mult, ALU.subtract).then_inc(y_lo_ready, 1)

            def make_pick(i):
                dve.tensor_tensor(pick[:, :, :, :].rearrange("p b x t -> p (b x) t"),
                                  c_(C_IOTA, P).unsqueeze(1).to_broadcast([P, 4, P]),
                                  slots[:, i, :, :].rearrange("p b x -> p (b x)").unsqueeze(2).to_broadcast([P, 4, P]),
                                  ALU.is_equal).then_inc(pick_ready, 1)

            def gather_rest(first):
                for r in range(4):
                    dve.wait_ge(xg_hi_ready, first + (r + 1))
                    dve.tensor_tensor(xg_lo[:, 2 * r:2 * r + 2, :], ps[(7, 4, 5, 4)[r]][:, :].rearrange("p (k t) -> p k t", k=2),
                                      xg_hi[:, 2 * r:2 * r + 2, :].bitcast(F32), ALU.subtract).then_inc(xg_lo_ready, 1)

            make_pick(0)
            dve.wait_ge(zeros_made, 3)
            gather_rest(0)
            n = dve.value_load(n_iter[0:1, 0:1], min_val=8, max_val=16)
            with dve.Fori(0, n) as it:
                for q in range(3):
                    ex_lo_(it, q)
                y_rest(1, 2 * it)
                for e in range(2):
                    for q in range(3, 11):
                        ex_lo_(it, 12 * e + q)
                    dve.wait_ge(ex_done, 24 * it + (12 * e + 12))
                    dve.wait_ge(act_g_ready, 2 * it + (e + 1))
                    dve.tensor_tensor(hid[:, :], act_g[:, :], ps[5][:, :], ALU.mult).then_inc(hid_ready, 1)
                    ex_lo_(it, 12 * e + 11)
                    dve.wait_ge(hid_hi_ready, 2 * it + (e + 1))
                    dve.tensor_tensor(hid_lo[:, :, :], ps[6][:, :].rearrange("p (f t) -> p f t", f=4),
                                      hid_hi[:, :, :].bitcast(F32), ALU.subtract).then_inc(hid_lo_ready, 1)
                    if e == 0:
                        dve.wait_ge(comb_mm, it + 1)
                        dve.tensor_copy(comb_slot[:, :], ps[4][:, 0:2]).then_inc(comb_ready, 1)
                        make_pick(it + 1)
                        for q in range(12, 15):
                            ex_lo_(it, q)
                        dve.wait_ge(comb_ready, it + 1)
                        y_rest(0, 2 * it + 1)
                    else:
                        gather_rest(4 * it + 4)
            y_rest(1, 2 * n)
            dve.wait_ge(moe_done, 1)
            for b in range(TB):
                for half in range(2):
                    dve.tensor_tensor(result[:, b, halves(half)], ps[2 * b + half][:, :], mod_rest[:, 3, halves(half)],
                                      ALU.mult).then_inc(fin, 1)
                for half in range(2):
                    dve.wait_ge(fin, 4 * b + half + 1)
                    dve.tensor_tensor(result[:, b, halves(half)], result[:, b, halves(half)], h[:, b, halves(half)],
                                      ALU.add).then_inc(fin, 1)
            dve.wait_ge(fin_sq, TB)
            dve.tensor_scalar(stat[:, 2:4], stat[:, 0:2], 1.0 / D, EPS, ALU.mult, ALU.add).then_inc(fin, 1)
            dve.wait_ge(fin_rms, 1)
            dve.reciprocal(stat[:, 2:4], stat[:, 2:4]).then_inc(fin, 1)
            dve.wait_ge(fin, 4 * TB + 2)
            for b in range(TB):
                dve.scalar_tensor_tensor(result[:, b, :], result[:, b, :], stat[:, 2 + b:3 + b], norm_rows[:, 1, :],
                                         ALU.mult, ALU.mult).then_inc(fin, 1)

        @block.gpsimd
        def _(pool):
            for i in range(4):
                r = slice(4 * i, 4 * i + 4)
                pool.wait_ge(gy_made, i + 1)
                pool.tensor_tensor(sq2[:, r, :], xl[:, r, :], xl[:, r, :], ALU.mult).then_inc(sq2_made, 1)


def kernel(**inputs):
    import numpy as np
    import concourse.bacc as bacc
    from concourse.bass_utils import run_bass_kernel_spmd

    nc, arrays, _ = prepare(inputs, np, bacc)
    r = run_bass_kernel_spmd(nc, [arrays], core_ids=[0])
    return r.results[0]["out"].reshape(1, T, D)


def prepare(inputs, np, bacc):
    i = {k: np.ascontiguousarray(v) for k, v in inputs.items()}

    def cols(v):
        return v.reshape(-1, P).T

    def tiles(w):
        k, n = w.shape
        return w.reshape(k // P, P, n // P, P).transpose(2, 1, 0, 3)

    par = np.zeros((P, C_END), np.float32)
    par[:, C_COND:C_COND + 16] = np.stack([cols(i["c"][0]), cols(i["c_ctx"])], -1).reshape(P, 16)
    par[:, C_BADA:C_BADA + 16] = cols(i["b_ada"][0, :2048])
    par[:, C_NMIX:C_NMIX + 8] = cols(i["norm_mix"][0])
    par[:, C_CW:C_CW + 96] = i["ssd_conv_w"][0].reshape(4, 24, P).transpose(2, 1, 0).reshape(P, 96)
    par[:, C_CB:C_CB + 24] = cols(i["ssd_conv_b"][0])
    par[:, C_SSDN:C_SSDN + 16] = cols(i["ssd_norm"][0])
    par[:, C_SCW:C_SCW + 24] = i["sc_conv_w"][0].reshape(3, 8, P).transpose(2, 1, 0).reshape(P, 24)
    par[:, C_DSKIP:C_DSKIP + 16] = cols(np.repeat(i["ssd_d"][0], 64))
    at = np.arange(P)
    par[:, C_IDENT:C_IDENT + P] = np.eye(P)
    par[:, C_ONES:C_ONES + P] = 1
    par[:, C_UP:C_UP + P] = at[None, :] >= at[:, None]
    par[:, C_LO:C_LO + P] = at[None, :] <= at[:, None]
    par[:, C_IOTA:C_IOTA + P] = at[None, :]
    tri = (np.arange(4)[None, :] < np.arange(4)[:, None]).reshape(16)
    par[:, C_TRI:C_TRI + 16] = tri
    par[:, C_NTRI:C_NTRI + 16] = ~tri
    w_in = i["w_in"][0]
    z, x, b, c, dt, sb, sc, sh, ma, mb = np.split(w_in, [2048, 4096, 4608, 5120, 5184, 6208, 7232, 8256, 9280], 1)
    units = [tiles(b), tiles(c), tiles(x), tiles(z),
             np.stack([tiles(sc), tiles(sh)], 1).reshape(16, P, KD, P), tiles(sb), tiles(mb), tiles(ma),
             tiles(i["w_sc_out"][0]),
             i["w_ssd_out"][0].reshape(2, KD, P, KD, P).transpose(3, 0, 2, 1, 4).reshape(16, P, KD, P),
             i["w_o"][0].reshape(KD, P, KD, P)]
    tokens = np.concatenate([i["ctx"][0], i["x"][0]])
    experts = np.stack([i["w_gate"][0].reshape(NE, KD, P, 512).transpose(0, 2, 1, 3),
                        i["w_up"][0].reshape(NE, KD, P, 512).transpose(0, 2, 1, 3),
                        i["w_down"][0].reshape(NE, 4, P, D).transpose(0, 2, 1, 3).reshape(NE, P, KD, 512)], 1)
    arrays = {
        "par": par,
        "head_rows": np.stack([i["ssd_dt_bias"][0].reshape(64), i["ssd_a_log"][0].reshape(64)], 1),
        "x_t": tokens.reshape(2 * T, KD, P).transpose(2, 1, 0),
        "x": i["x"][0],
        "w_ada": i["w_ada"][0].reshape(KD, P, 12, 512).transpose(2, 1, 0, 3),
        "b_ada_rest": i["b_ada"][0, 2048:].reshape(1, 4096),
        "w_dt": dt.reshape(KD, P, 64).transpose(1, 0, 2),
        "units": np.concatenate(units),
        "w_router": i["w_router"].reshape(KD, P, NE).transpose(1, 0, 2),
        "rows": np.stack([i["norm_ffn"][0], i["final_norm"]]),
        "b_router": i["b_router"].reshape(1, NE),
        "experts": experts.reshape(3 * NE, P, KD, 512),
    }
    arrays = {k: np.ascontiguousarray(v) for k, v in arrays.items()}
    nc = bacc.Bacc("TRN2", target_bir_lowering=False, num_devices=1)
    a = {k: nc.dram_tensor(k, v.shape, F32, kind="ExternalInput").ap() for k, v in arrays.items()}
    out = nc.dram_tensor("out", (T, D), F32, kind="ExternalOutput").ap()
    scratch = nc.dram_tensor("ada_scratch", (1, 4096), F32, kind="Internal").ap()
    build(nc, a, out, scratch)
    return nc, arrays, out
```

```python
from contextlib import ExitStack

import concourse.bass as bass
from concourse import mybir

F32 = mybir.dt.float32
F32R = mybir.dt.float32r
I32 = mybir.dt.int32
ALU = mybir.AluOpType
ACT = mybir.ActivationFunctionType
AX_X = mybir.AxisListType.X

P = 128
D = 1024
KD = D // P
T = 256
TB = T // P
INNER = 2048
HEADS = 32
GROUPS = 4
NE = 16
EPS = 1e-6

U_DT = 0
U_B = 1
U_C = 5
U_X = 9
U_Z = 25
U_CH = 41
U_GATEB = 57
U_MB = 65
U_MA = 73
U_SC = 81
U_SSD = 89
U_O = 105
U_END = 113
RAW = 4

C_COND, C_BADA, C_NMIX, C_CW, C_CB, C_SSDN, C_SCW, C_DSKIP, C_IDENT = 0, 16, 32, 40, 136, 160, 176, 200, 216
C_ONES, C_UP, C_LO, C_IOTA, C_TRI, C_NTRI, C_PICK2, C_END = 344, 472, 600, 728, 856, 872, 888, 952

ADA_ORDER = (0, 2, 1, 3)
DT_AT = [0, 4, 8, 12, 14, 18, 22, 30]
DT_REV, DT_DONE = 30, 31
SOFTPLUS_AT = {3: (0,), 4: (1, 2), 6: (3,), 7: (4,), 8: (5,), 10: (6,), 17: (7,)}
LOG1P = [1.0 / (2 * j + 1) for j in range(8)]


def first_unit_of_step(s):
    return U_CH + min(s, 32) * 40 // 32


def build(nc, a, out, scratch):
    with ExitStack() as ctx:
        base = 16512
        ctx.enter_context(nc.sbuf_tensor("arena", [P, 53000], F32))

        def at(name, kib, shape, dt=F32):
            return nc.alloc_sbuf_tensor_at(name, shape, dt, offset=base + int(kib * 1024))

        def sem(name):
            return ctx.enter_context(nc.semaphore(name))

        ps = [ctx.enter_context(nc.psum_tensor(f"ps{i}", [P, 512], F32)) for i in range(8)]

        par = at("par", 0, [P, C_END])
        headrow = at("headrow", 204.0625, [64, 2])
        a_pos = at("a_pos", 204.125, [64, 1])
        u_hi = at("u_hi", 4, [P, 2, KD, T], F32R)
        u_lo = at("u_lo", 20, [P, 2, KD, T], F32R)
        raw = at("raw", 36, [P, RAW, KD, P])
        w_hi = [at(f"w_hi{i}", 52 + 4 * i, [P, KD, P], F32R) for i in range(2)]
        w_lo = [at(f"w_lo{i}", 60 + 4 * i, [P, KD, P], F32R) for i in range(2)]
        x_in = at("x_in", 108, [P, KD, 2 * T])
        x_sq = at("x_sq", 148, [P, KD, 2 * T])
        mean_sq = at("mean_sq", 132, [P, 2 * T])
        rms_in = at("rms_in", 134, [P, 2 * T])
        rstd_in = at("rstd_in", 136, [P, 2 * T])
        cond = at("cond", 138, [P, KD, 2])
        mod_col = at("mod_col", 138.25, [P, 16, 2])
        gain_col = at("gain_col", 138.5, [P, KD, 2])
        mod_row = at("mod_row", 68, [2, 2048])
        wa = [at(f"wa{i}", kib, [P, KD, 512]) for i, kib in enumerate((92, 168, 4, 76))]
        ada_sum = at("ada_sum", 132, [P, 8, 512])
        cond_keep = at("cond_keep", 204, [P, KD])
        conv = [at(f"conv{i}", 88 + 2 * i, [P, 2, T]) for i in range(2)]
        dt_r = at("dt_r", 76, [64, 512])
        dt_e = at("dt_e", 78, [64, 512])
        dt_t = at("dt_t", 80, [64, 512])
        dt_t2 = at("dt_t2", 82, [64, 512])
        dt_q = at("dt_q", 84, [64, 512])
        dt = at("dt", 86, [64, 4, P])
        rev = at("rev", 68, [64, 4, P])
        w_ctx = at("w_ctx", 70, [64, 2, P])
        dec_t = at("dec_t", 71, [64, 2, P])
        coef_t = at("coef_t", 72, [64, 2, P])
        cum = at("cum", 187.5, [64, 4, P])
        tok = at("tok", 185, [P, 2, 4, 64])
        coef = at("coef", 187, [P, 2, 64])
        vc = at("vc", 68, [P, KD, T])
        v_tmp = [at(f"v_tmp{i}", 202 + i, [P, T]) for i in range(2)]
        gb_hi = at("gb_hi", 4, [P, KD, T], F32R)
        gb_lo = at("gb_lo", 20, [P, KD, T], F32R)
        gb_tmp = [at(f"gb_tmp{i}", 204.25 + i, [P, T]) for i in range(2)]
        m_a = at("m_a", 76, [P, KD, T])
        m_b = at("m_b", 84, [P, KD, T])
        z = at("z", 92, [P, 16, T])
        xl = at("xl", 108, [P, 16, T])
        bl = at("bl", 124, [P, GROUPS, T])
        cl = at("cl", 128, [P, GROUPS, T])
        xc = at("xc", 148, [P, 16, T])
        bc = at("bc", 164, [P, GROUPS, T])
        state = at("state", 132, [P, GROUPS, 2, 512])
        xw = at("xw", 190, [P, 2, 2, 512])
        b_tok = at("b_tok", 198, [P, 2 * GROUPS, P])
        xn = [at(f"xn{i}", 148 + 4 * i, [P, 2, 512]) for i in range(2)]
        cb_up = [at(f"cb_up{i}", 156 + 3 * i, [P, 2, P]) for i in range(2)]
        cb_lo = [at(f"cb_lo{i}", 157 + 3 * i, [P, 2, P]) for i in range(2)]
        cb_off = [at(f"cb_off{i}", 158 + 3 * i, [P, 2, P]) for i in range(2)]
        yi = [at(f"yi{i}", 162 + 4 * i, [P, 2, 512]) for i in range(2)]
        yi_tmp = at("yi_tmp", 170, [P, 512])
        back = at("back", 172, [P, 2, P])
        expo = at("expo", 173, [P, 2, P])
        dec = [at(f"dec{i}", 174 + 2 * i, [P, 4, P]) for i in range(2)]
        wd_tmp = at("wd_tmp", 178, [P, 2, P])
        wd = [at(f"wd{i}", 179 + i, [P, 2, P]) for i in range(2)]
        mix = [at(f"mix{i}", 181 + 2 * i, [P, 4, P]) for i in range(2)]

        cum_r = at("cum_r", 190, [P, 2, P], F32R)
        cum_rest = at("cum_rest", 191, [P, 2, P])
        pick2 = at("pick2", 189.5, [P, 64], F32R)

        gy_sq = at("gy_sq", 192, [P, T])
        sq_all = at("sq_all", 193, [P, T])
        gg_hi = at("gg_hi", 92, [P, 16, T], F32R)
        gg_lo = at("gg_lo", 132, [P, 16, T], F32R)
        m_hi = at("m_hi", 164, [P, KD, T], F32R)
        m_lo = at("m_lo", 172, [P, KD, T], F32R)
        merged = [at(f"merged{i}", 180 + i, [P, T]) for i in range(2)]
        rstd2 = at("rstd2", 182, [P, T])
        rms2 = at("rms2", 183, [P, T])
        b_row = at("b_row", 168, [1, 4096])
        mod_rest = at("mod_rest", 108, [P, 4, D])
        norm_rows = at("norm_rows", 124, [P, 2, D])
        x_nat = at("x_nat", 68, [P, TB, D])
        h = at("h", 12, [P, TB, D])
        u2 = at("u2", 28, [P, TB, D])
        u2_hi = at("u2_hi", 4, [P, TB, D], F32R)
        u2_lo = at("u2_lo", 20, [P, TB, D], F32R)
        u2_t = at("u2_t", 76, [P, KD, T])
        w_rt = at("w_rt", 196, [P, KD, NE])
        b_rt = at("b_rt", 196.5, [P, NE])
        stat = at("stat", 196.75, [P, 8])
        n_iter = at("n_iter", 196.8125, [1, 2], I32)
        cmp_gt = at("cmp_gt", 197, [P, 8, 4, 4])
        cmp_ge = at("cmp_ge", 197.5, [P, 8, 4, 4])
        score = at("score", 198, [P, TB, NE])
        sel = at("sel", 198.125, [P, TB, NE])
        rank = at("rank", 198.25, [P, 8, 4])
        top2 = at("top2", 198.375, [P, 8, 4])
        g_score = at("g_score", 198.5, [P, 8])
        g_rank = at("g_rank", 198.5625, [P, 8])
        chosen = at("chosen", 198.625, [P, TB, NE])
        comb = at("comb", 198.75, [P, TB, NE])
        slot = at("slot", 198.875, [P, TB, NE])
        sel_top = at("sel_top", 199, [P, 8, 4])
        slots = at("slots", 199.25, [P, 17, TB, 2])
        combs = at("combs", 199.75, [P, 16, TB, 2])
        comb_slot = at("comb_slot", 200.25, [P, 2])
        ex_raw = [at(f"ex_raw{i}", 132 + 16 * i, [P, KD, 512]) for i in range(3)]
        ex_hi = [at(f"ex_hi{i}", 36 + 4 * i, [P, 2, 512], F32R) for i in range(4)]
        ex_lo = [at(f"ex_lo{i}", 52 + 4 * i, [P, 2, 512], F32R) for i in range(4)]
        xg_hi = at("xg_hi", 76, [P, KD, 2 * P], F32R)
        xg_lo = at("xg_lo", 84, [P, KD, 2 * P], F32R)
        y_hi = at("y_hi", 92, [P, D], F32R)
        y_lo = at("y_lo", 96, [P, D], F32R)
        pick = at("pick", 100, [P, TB, 2, P], F32R)
        put = at("put", 102, [P, 2, TB, P], F32R)
        act_g = at("act_g", 104, [P, 512])
        hid = at("hid", 106, [P, 512])
        hid_hi = at("hid_hi", 68, [P, 4, P], F32R)
        hid_lo = at("hid_lo", 70, [P, 4, P], F32R)
        zero_r = at("zero_r", 72, [P, 512], F32R)
        result = at("result", 28, [P, TB, D])

        def c_(i, n=1):
            return par[:, i:i + n]

        ident = c_(C_IDENT, P)
        ones = c_(C_ONES, P)

        par_in = sem("par_in")
        x_loaded = sem("x_loaded")
        headrow_in = sem("headrow_in")
        raw_full = [sem(f"raw_full{i}") for i in range(RAW)]
        wa_full = [sem(f"wa_full{i}") for i in range(4)]
        cond_ready = sem("cond_ready")
        sq_ready = sem("sq_ready")
        sq_sum = sem("sq_sum")
        ms_done = sem("ms_done")
        ms_read = sem("ms_read")
        rms_ready = sem("rms_ready")
        xn_chain = sem("xn_chain")
        ada_mm = sem("ada_mm")
        mod_row_ready = sem("mod_row_ready")
        mod_tp = sem("mod_tp")
        mod_ready = sem("mod_ready")
        u_ctx = sem("u_ctx")
        u_lat = sem("u_lat")
        u_hi_ready = sem("u_hi_ready")
        u_lo_ready = sem("u_lo_ready")
        split_hi = sem("split_hi")
        split_lo = sem("split_lo")
        unit_done = sem("unit_done")
        dt_read = sem("dt_read")
        copied = sem("copied")
        v_made = sem("v_made")
        gated = sem("gated")
        gb_hi_ready = sem("gb_hi_ready")
        gb_lo_ready = sem("gb_lo_ready")
        carry_chain = sem("carry_chain")
        wd_ready = sem("wd_ready")
        conv_init = sem("conv_init")
        conv_tap = sem("conv_tap")
        conv_done = sem("conv_done")
        act_dt = sem("act_dt")
        dve_dt = sem("dve_dt")
        ada_acc = sem("ada_acc")
        ada_summed = sem("ada_summed")
        ada_row_ready = sem("ada_row_ready")
        ada_stored = sem("ada_stored")
        piece = sem("piece")
        piece_act = sem("piece_act")
        piece_dve = sem("piece_dve")
        v_chain = sem("v_chain")
        cum_hi_ready = sem("cum_hi_ready")
        cum_lo_ready = sem("cum_lo_ready")
        cum_r_in = sem("cum_r_in")
        rows_done = sem("rows_done")
        expo_ready = sem("expo_ready")
        scan_chain = sem("scan_chain")
        dec_ready = sem("dec_ready")
        mix_ready = sem("mix_ready")
        y_done = sem("y_done")
        y_stored = sem("y_stored")
        b_row_in = sem("b_row_in")
        sig_ready = sem("sig_ready")
        gy_made = sem("gy_made")
        sq_step = sem("sq_step")
        ssq_done = sem("ssq_done")
        ms2_ready = sem("ms2_ready")
        rms2_ready = sem("rms2_ready")
        ma_scaled = sem("ma_scaled")
        gg_hi_ready = sem("gg_hi_ready")
        gg_lo_ready = sem("gg_lo_ready")
        branch_b = sem("branch_b")
        merge_chain = sem("merge_chain")
        merge_made = sem("merge_made")
        m_hi_ready = sem("m_hi_ready")
        m_lo_ready = sem("m_lo_ready")
        mod_rest_in = sem("mod_rest_in")
        norm_rows_in = sem("norm_rows_in")
        x_nat_in = sem("x_nat_in")
        w_rt_in = sem("w_rt_in")
        b_rt_in = sem("b_rt_in")
        nf_made = sem("nf_made")
        h_scaled = sem("h_scaled")
        h_ready = sem("h_ready")
        h_sq = sem("h_sq")
        h_ms = sem("h_ms")
        h_rms = sem("h_rms")
        u2_chain = sem("u2_chain")
        u2_hi_ready = sem("u2_hi_ready")
        u2_lo_ready = sem("u2_lo_ready")
        u2_tp = sem("u2_tp")
        u2_t_act = sem("u2_t_act")
        u2_t_dve = sem("u2_t_dve")
        logits_done = sem("logits_done")
        score_ready = sem("score_ready")
        route = sem("route")
        positions = sem("positions")
        ex_full = [sem(f"ex_full{i}") for i in range(3)]
        ex_hi_ready = sem("ex_hi_ready")
        ex_lo_ready = sem("ex_lo_ready")
        ex_done = sem("ex_done")
        zeros_made = sem("zeros_made")
        acc_started = sem("acc_started")
        pick_ready = sem("pick_ready")
        gathered = sem("gathered")
        xg_hi_ready = sem("xg_hi_ready")
        xg_lo_ready = sem("xg_lo_ready")
        act_g_ready = sem("act_g_ready")
        hid_ready = sem("hid_ready")
        hid_tp = sem("hid_tp")
        hid_hi_ready = sem("hid_hi_ready")
        hid_lo_ready = sem("hid_lo_ready")
        put_tp = sem("put_tp")
        put_ready = sem("put_ready")
        comb_mm = sem("comb_mm")
        comb_ready = sem("comb_ready")
        y_hi_ready = sem("y_hi_ready")
        y_lo_ready = sem("y_lo_ready")
        scattered = sem("scattered")
        moe_done = sem("moe_done")
        fin = sem("fin")
        fin_sq = sem("fin_sq")
        fin_rms = sem("fin_rms")
        out_stored = sem("out_stored")

        def freed(u):
            if u == U_DT:
                return dt_read, 1
            if u < U_Z:
                return conv_tap, 3 * (u - U_B) + 3
            if u < U_CH:
                return copied, u - U_Z + 1
            if u < U_GATEB:
                i = (u - U_CH) // 2
                return (copied, 16 + i + 1) if (u - U_CH) % 2 == 0 else (v_made, i + 1)
            if u < U_MB:
                return gated, u - U_GATEB + 1
            if u < U_SC:
                return copied, 24 + (u - U_MB) + 1
            return branch_b, u - U_SC + 1

        PIECES = [("tables", 0), ("b_ctx", 0)]
        for g in range(GROUPS):
            PIECES += [("x_ctx", g), ("state", g)]
        for g in range(GROUPS):
            PIECES += [("x_lat", g), ("cb", g), ("carry", 2 * g), ("carry", 2 * g + 1)]
        BY_ACT = ("tables", "b_ctx", "state", "x_lat", "cb")
        BY_DVE = ("tables", "x_ctx", "cb", "carry")

        def act_pieces(n):
            return sum(k in BY_ACT for k, _ in PIECES[:n])

        def dve_pieces(n):
            return sum(k in BY_DVE for k, _ in PIECES[:n])

        FIRST_PIECE_UNIT = U_Z + 1

        def piece_at_unit(u):
            n = u - FIRST_PIECE_UNIT
            return n if 0 <= n < 14 else None

        def piece_at_step(s):
            g, k = s // 8, s % 8 - 1
            return 10 + 4 * (g + 1) + k if g < GROUPS - 1 and 0 <= k < 4 else None

        SQ_DONE = 31
        ROUTE_CHOSEN, ROUTE_READ, ROUTE_N = 18, 27, 31
        FIN_OUT = 11

        def tiles_gated(s):
            return min(max((s - 2) // 2, 0), 16)

        block = ctx.enter_context(nc.Block())

        @block.sync
        def _(sp):
            sp.dma_start(par[:, :], a["par"]).then_inc(par_in, 16)
            def load_wa(j):
                slot = j if j < 4 else j % 2
                if 4 <= j < 6:
                    sp.wait_ge(ada_mm, j - 3)
                if j >= 6:
                    sp.wait_ge(ada_acc, 8 * (j - 5))
                sp.dma_start(wa[slot][:, :, :], a["w_ada"][ADA_ORDER[j] if j < 4 else j]).then_inc(wa_full[slot], 16)

            def load_unit(u):
                if u >= RAW:
                    sp.wait_ge(split_lo, u - RAW + 1)
                if u == U_DT:
                    sp.dma_start(raw[:, 0, :, 0:64], a["w_dt"]).then_inc(raw_full[0], 16)
                else:
                    sp.dma_start(raw[:, u % RAW, :, :], a["units"][u - 1]).then_inc(raw_full[u % RAW], 16)

            load_wa(0)
            sp.dma_start(x_in[:, :, :], a["x_t"]).then_inc(x_loaded, 16)
            load_wa(1)
            load_wa(2)
            load_unit(U_DT)
            load_wa(3)
            sp.dma_start(headrow[:, :], a["head_rows"]).then_inc(headrow_in, 16)
            for u in range(1, RAW):
                load_unit(u)
            for j in range(4, 6):
                load_wa(j)
            for u in range(RAW, U_SC):
                load_unit(u)
                if u in range(U_X + 5, U_X + 17, 2):
                    load_wa(6 + (u - U_X - 5) // 2)
                if u == U_Z + 2:
                    sp.wait_ge(ada_acc, 64)
                    sp.dma_start(b_row[:, :], a["b_ada_rest"]).then_inc(b_row_in, 16)
                if u == U_Z + 5:
                    sp.wait_ge(ada_row_ready, 8)
                    sp.dma_start(scratch, b_row[:, :]).then_inc(ada_stored, 16)
            for u in range(U_SC, U_END):
                load_unit(u)
                if u == U_SSD + 3:
                    sp.wait_ge(y_done, HEADS)
                    sp.wait_ge(gb_lo_ready, KD)
                    sp.dma_start(norm_rows[:, :, :], a["rows"].unsqueeze(0).to_broadcast([P, 2, D])).then_inc(norm_rows_in, 16)
                    sp.dma_start(x_nat[:, :, :], a["x"].rearrange("(b p) d -> p b d", p=P)).then_inc(x_nat_in, 16)
                    sp.dma_start(w_rt[:, :, :], a["w_router"]).then_inc(w_rt_in, 16)
                    sp.dma_start(b_rt[:, :], a["b_router"].to_broadcast([P, NE])).then_inc(b_rt_in, 16)
                if u == U_SSD + 4:
                    sp.wait_ge(ada_stored, 16)
                    sp.wait_ge(sq_step, SQ_DONE)
                    sp.wait_ge(gg_lo_ready, 16)
                    sp.dma_start(mod_rest[:, :, :], scratch.rearrange("a (k d) -> a k d", k=4).to_broadcast([P, 4, D]))\
                      .then_inc(mod_rest_in, 16)

            def load_expert(x, index):
                for m in range(3):
                    sp.wait_ge(ex_lo_ready, 12 * x + 4 * m + 4)
                    sp.dma_start(ex_raw[m][:, :, :], a["experts"][3 * index + m]).then_inc(ex_full[m], 16)

            for m in range(3):
                if m == 0:
                    sp.wait_ge(unit_done, U_O)
                elif m == 1:
                    sp.wait_ge(ssq_done, 1)
                else:
                    sp.wait_ge(unit_done, U_END)
                sp.dma_start(ex_raw[m][:, :, :], a["experts"][m]).then_inc(ex_full[m], 16)
            with sp.Fori(0, 7) as pair:
                load_expert(2 * pair + 1, 2 * pair + 1)
                load_expert(2 * pair + 2, 2 * pair + 2)
            load_expert(15, 15)
            sp.wait_ge(route, ROUTE_N)
            n = sp.value_load(n_iter[0:1, 0:1], min_val=8, max_val=16)
            with sp.If(n > 8):
                with sp.Fori(0, 8) as pair:
                    load_expert(2 * pair + 16, 2 * pair)
                    load_expert(2 * pair + 17, 2 * pair + 1)
            for b in range(TB):
                sp.wait_ge(fin, FIN_OUT + 3 * b)
                sp.dma_start(out[b * P:(b + 1) * P, :], result[:, b, :]).then_inc(out_stored, 16)
            sp.wait_ge(out_stored, 16 * TB)

        @block.tensor
        def _(pe):
            pe.wait_ge(par_in, 16)
            pe.wait_ge(cond_ready, 1)
            def mod_columns(half):
                pe.wait_ge(mod_row_ready, 2 * half + 2)
                if half:
                    pe.wait_ge(mod_ready, 1)
                for t in range(16):
                    if t % 8 // 4 == half:
                        mm = pe.transpose(ps[5][:, 2 * t:2 * t + 2], mod_row[0:2, t * P:(t + 1) * P],
                                          par[0:2, C_IDENT:C_IDENT + 2])
                mm.then_inc(mod_tp, 1)

            for n, j in enumerate(ADA_ORDER):
                if n == 2:
                    pe.wait_ge(sq_sum, 4)
                    pe.matmul(ps[0][:, :], ones, x_sq[:, 0, :], start=True, stop=True).then_inc(ms_done, 1)
                pe.wait_ge(wa_full[n], 16)
                for k in range(KD):
                    mm = pe.matmul(ps[1 + j][0:2, :], cond[:, k, :], wa[n][:, k, :],
                                   start=k == 0, stop=k == KD - 1)
                mm.then_inc(ada_mm, 1)
                if n == 2:
                    mod_columns(0)

            def dt_unit():
                out_ap = ps[0][0:64, :]
                pe.wait_ge(ms_read, 1)
                pe.wait_ge(split_hi, 1)
                for half in range(2):
                    tiles = range(4 * half, 4 * half + 4)
                    for k in tiles:
                        pe.wait_ge(u_hi_ready, 2 * k + 2)
                        pe.wait_ge(u_lo_ready, k + 1)
                        pe.matmul(out_ap, w_hi[0][:, k, 0:64], u_hi[:, :, k, :], start=k == 0, stop=False)
                        pe.matmul(out_ap, w_hi[0][:, k, 0:64], u_lo[:, :, k, :], start=False, stop=False)
                    if half == 0:
                        mod_columns(1)
                        pe.wait_ge(split_lo, 1)
                    for k in tiles:
                        mm = pe.matmul(out_ap, w_lo[0][:, k, 0:64], u_hi[:, :, k, :], start=False, stop=k == KD - 1)
                mm.then_inc(unit_done, 1)

            def unit(u, out_ap, hi, lo, first=True, last=True):
                pe.wait_ge(split_hi, u + 1)
                wh, wl = w_hi[u % 2], w_lo[u % 2]
                for k in range(KD):
                    pe.matmul(out_ap, wh[:, k, :], hi(k), start=first and k == 0, stop=False)
                    pe.matmul(out_ap, wh[:, k, :], lo(k), start=False, stop=False)
                pe.wait_ge(split_lo, u + 1)
                for k in range(KD):
                    mm = pe.matmul(out_ap, wl[:, k, :], hi(k), start=False, stop=last and k == KD - 1)
                mm.then_inc(unit_done, 1)

            def in_unit(u):
                if u >= 2:
                    pe.wait_ge(*freed(u - 2))
                bank = ps[u % 2]
                if u == U_DT:
                    dt_unit()
                elif U_C <= u < U_X or u >= U_Z:
                    unit(u, bank[:, 0:T], lambda k: u_hi[:, 1, k, :], lambda k: u_lo[:, 1, k, :])
                else:
                    unit(u, bank[:, :], lambda k: u_hi[:, :, k, :], lambda k: u_lo[:, :, k, :])

            def transposes(bank, cols, src):
                for i, s in enumerate(src):
                    mm = pe.transpose(bank[:, i * cols:(i + 1) * cols], s, par[0:cols, C_IDENT:C_IDENT + cols])
                return mm

            def run_piece(n):
                kind, g = PIECES[n]
                if n and act_pieces(n):
                    pe.wait_ge(piece_act, act_pieces(n))
                if n and dve_pieces(n):
                    pe.wait_ge(piece_dve, dve_pieces(n))
                b6, b7 = ps[6], ps[7]
                if kind == "tables":
                    pe.wait_ge(dve_dt, DT_DONE)
                    pe.wait_ge(act_dt, 8)
                    src = []
                    for b in range(2):
                        src += [cum[:, 2 + b, :], dt[:, 2 + b, :], rev[:, 2 + b, :], dec_t[:, b, :]]
                    transposes(b6, 64, src)
                    mm = transposes(b7, 64, [coef_t[:, b, :] for b in range(2)])
                elif kind == "b_ctx":
                    pe.wait_ge(conv_done, 24)
                    transposes(b6, P, [bc[:, i // 2, (i % 2) * P:(i % 2 + 1) * P] for i in range(4)])
                    mm = transposes(b7, P, [bc[:, i // 2, (i % 2) * P:(i % 2 + 1) * P] for i in range(4, 8)])
                elif kind == "x_ctx":
                    for b in range(2):
                        mm = transposes(ps[6 + b], P, [xc[:, 4 * g + t, b * P:(b + 1) * P] for t in range(4)])
                elif kind == "state":
                    for d in range(2):
                        for b in range(2):
                            mm = pe.matmul(ps[6 + d][:, :], b_tok[:, 2 * g + b, :], xw[:, b, d, :],
                                           start=b == 0, stop=b == 1)
                elif kind == "x_lat":
                    for b in range(2):
                        mm = transposes(ps[6 + b], P, [xl[:, 4 * g + t, b * P:(b + 1) * P] for t in range(4)])
                elif kind == "cb":
                    for i, (s, l) in enumerate(((0, 0), (0, 1), (1, 1), (1, 0))):
                        mm = pe.matmul(b7[:, i * P:(i + 1) * P], bl[:, g, s * P:(s + 1) * P], cl[:, g, l * P:(l + 1) * P],
                                       start=True, stop=True)
                else:
                    gg, l = g // 2, g % 2
                    for d in range(2):
                        mm = pe.matmul(ps[6 + d][:, :], cl[:, gg, l * P:(l + 1) * P], state[:, gg, d, :],
                                       start=True, stop=True)
                mm.then_inc(piece, 1)

            def sum_ada():
                for j in range(8):
                    pe.wait_ge(ada_acc, 8 * j + 8)
                    if j >= 2:
                        pe.wait_ge(ada_row_ready, j - 1)
                    pe.matmul(ps[2 + j % 2][0:1, :], ones[:, 0:1], ada_sum[:, j, :],
                              start=True, stop=True).then_inc(ada_summed, 1)

            for u in range(U_CH):
                in_unit(u)
                if u == U_Z + 1:
                    sum_ada()
                if piece_at_unit(u) is not None:
                    run_piece(piece_at_unit(u))

            def head_rows(h):
                if h == 0:
                    pe.wait_ge(ada_row_ready, 8)
                    pe.wait_ge(cum_hi_ready, 3)
                if h >= 2:
                    pe.wait_ge(dec_ready, h - 1)
                for d in range(2):
                    mm = pe.matmul(ps[2 + h % 2][:, d * T:(d + 1) * T],
                                   pick2[:, 32 * d + h:32 * d + h + 1].to_broadcast([P, P]),
                                   cum_r[:, :, :], start=d == 0, stop=d == 1, skip_group_check=True)
                mm.then_inc(rows_done, 1)

            def y_head(h):
                g, pair, j = h // 8, h // 2, h % 2
                bank = ps[4 + pair % 2]
                if j == 0:
                    if pair >= 2:
                        pe.wait_ge(y_stored, pair - 1)
                    n = 10 + 4 * (g + 1)
                    pe.wait_ge(piece_dve, dve_pieces(n))
                    pe.wait_ge(piece_act, act_pieces(n))
                    for l in range(2):
                        pe.matmul(bank[:, l * P:(l + 1) * P], yi[g % 2][:, l, (pair % 4) * P:(pair % 4 + 1) * P], ident,
                                  start=l == 0, stop=False, skip_group_check=True)
                pe.wait_ge(mix_ready, h + 1)
                hh = h % 8
                for b in range(2):
                    mm = pe.matmul(bank[64 * j:64 * j + 64, 0:T], xn[g % 2][:, b, 64 * hh:64 * hh + 64],
                                   mix[h % 2][:, 2 * b:2 * b + 2, :], start=False, stop=j == 1 and b == 1,
                                   skip_group_check=True)
                mm.then_inc(y_done, 1)

            def branch_unit(u):
                pe.wait_ge(gb_lo_ready, KD)
                pe.wait_ge(*freed(u - 2))
                unit(u, ps[u % 2][:, 0:T], lambda k: gb_hi[:, k, :], lambda k: gb_lo[:, k, :])

            for s in range(HEADS + 2):
                if s < HEADS:
                    head_rows(s)
                for u in range(first_unit_of_step(s), first_unit_of_step(s + 1)):
                    in_unit(u)
                if s >= 2:
                    y_head(s - 2)
                if piece_at_step(s) is not None:
                    run_piece(piece_at_step(s))
                if s >= HEADS:
                    branch_unit(U_SC + s - HEADS)

            for u in range(U_SC + 2, U_SSD):
                if u == U_SC + 4:
                    pe.wait_ge(sq_step, SQ_DONE)
                    pe.matmul(ps[6][:, 0:T], ones, sq_all[:, :], start=True, stop=True).then_inc(ssq_done, 1)
                branch_unit(u)
            pe.wait_ge(gg_lo_ready, 16)
            pe.wait_ge(branch_b, KD)
            for n in range(KD):
                if n >= 2:
                    pe.wait_ge(merge_made, n - 1)
                for half in range(2):
                    unit(U_SSD + 2 * n + half, ps[n % 2][:, 0:T], lambda k: gg_hi[:, 8 * half + k, :],
                         lambda k: gg_lo[:, 8 * half + k, :], first=half == 0, last=half == 1)
            pe.wait_ge(y_stored, 16)
            for k in range(KD):
                u = U_O + k
                pe.wait_ge(m_lo_ready, k + 1)
                pe.wait_ge(split_hi, u + 1)
                pe.wait_ge(split_lo, u + 1)
                for b in range(TB):
                    for half in range(2):
                        bank = ps[2 + 2 * b + half][:, :]
                        wh, wl = (w[u % 2][:, 4 * half:4 * half + 4, :] for w in (w_hi, w_lo))
                        mh, ml = (m[:, k, b * P:(b + 1) * P] for m in (m_hi, m_lo))
                        pe.matmul(bank, mh, wh, start=k == 0, stop=False)
                        pe.matmul(bank, ml, wh, start=False, stop=False)
                        mm = pe.matmul(bank, mh, wl, start=False, stop=k == KD - 1)
                mm.then_inc(unit_done, 1)
            pe.sem_inc(ex_done, 4)
            pe.sem_inc(scattered, 1)
            pe.wait_ge(merge_made, KD)
            for b in range(TB):
                pe.wait_ge(u2_chain, 2 * b + 2)
                for k in range(KD):
                    mm = pe.transpose(ps[(0, 6)[b] + k // 4][:, (k % 4) * P:(k % 4 + 1) * P], u2[:, b, k * P:(k + 1) * P], ident)
                mm.then_inc(u2_tp, 1)
            pe.wait_ge(w_rt_in, 16)
            for b in range(TB):
                pe.wait_ge(u2_t_act, 2 if b == 0 else 3)
                if b == 1:
                    pe.wait_ge(u2_t_dve, 1)
                for k in range(KD):
                    mm = pe.matmul(ps[2][:, b * NE:(b + 1) * NE], u2_t[:, k, b * P:(b + 1) * P], w_rt[:, k, :],
                                   start=k == 0, stop=k == KD - 1)
            mm.then_inc(logits_done, 1)
            pe.wait_ge(route, ROUTE_CHOSEN)
            up = c_(C_UP, P)
            pe.matmul(ps[3][:, 0:NE], up, chosen[:, 0, :], start=True, stop=True)
            for o, second in ((NE, up), (2 * NE, ones)):
                pe.matmul(ps[3][:, o:o + NE], ones, chosen[:, 0, :], start=True, stop=False)
                mm = pe.matmul(ps[3][:, o:o + NE], second, chosen[:, 1, :], start=False, stop=True)
            mm.then_inc(positions, 1)

            def gather_round(first, r):
                bank = ps[(7, 4, 5, 4)[r]]
                if r == 3:
                    pe.wait_ge(xg_lo_ready, first + 2)
                for j in range(2):
                    k = 2 * r + j
                    for n_mm, (x, b) in enumerate(((u2_hi, 0), (u2_hi, 1), (u2_lo, 0), (u2_lo, 1))):
                        mm = pe.matmul(bank[:, j * 2 * P:(j + 1) * 2 * P], x[:, b, k * P:(k + 1) * P], pick[:, b, :, :],
                                       start=n_mm == 0, stop=n_mm == 3)
                mm.then_inc(gathered, 1)

            def scatter(put_e, b):
                for half in range(2):
                    for y in (y_hi, y_lo):
                        mm = pe.matmul(ps[2 * b + half][:, :], put[:, put_e, b, :], y[:, half * 512:(half + 1) * 512],
                                       start=False, stop=False, skip_group_check=True)
                return mm

            pe.wait_ge(zeros_made, 1)
            pe.wait_ge(route, ROUTE_READ)
            zr = zero_r[:, 0:P]
            for i in (0, 1, 2, 3, 6):
                mm = pe.matmul(ps[i][:, :], zr, zero_r[:, :], start=True, stop=i > 3, skip_group_check=i <= 3)
            mm.then_inc(acc_started, 1)
            pe.wait_ge(u2_hi_ready, TB)
            pe.wait_ge(u2_lo_ready, TB)
            pe.wait_ge(pick_ready, 1)
            for r in range(4):
                gather_round(0, r)
            pe.wait_ge(route, ROUTE_N)
            n = pe.value_load(n_iter[0:1, 0:1], min_val=8, max_val=16)
            with pe.Fori(0, n) as it:
                for e in range(2):
                    for m in range(2):
                        bank = ps[4 + m][:, :]
                        if e == 0:
                            pe.wait_ge(xg_lo_ready, 4 * it + 4)
                        else:
                            pe.wait_ge(*((put_ready, it + 1) if m == 0 else (comb_ready, it + 1)))
                        for q in range(4):
                            uq = 12 * e + 4 * m + q
                            pe.wait_ge(ex_hi_ready, 24 * it + uq + 1)
                            pe.wait_ge(ex_lo_ready, 24 * it + (uq + 1 + 12))
                            wh, wl = ex_hi[uq % 4], ex_lo[uq % 4]
                            for j in range(2):
                                k = 2 * q + j
                                xh, xlo = (x[:, k, e * P:(e + 1) * P] for x in (xg_hi, xg_lo))
                                pe.matmul(bank, xh, wh[:, j, :], start=k == 0, stop=False)
                                pe.matmul(bank, xlo, wh[:, j, :], start=False, stop=False)
                                mm = pe.matmul(bank, xh, wl[:, j, :], start=False, stop=k == KD - 1)
                            mm.then_inc(ex_done, 1)
                    pe.wait_ge(y_lo_ready, 4 * it + (2 * e + 2))
                    scatter(1 - e, 0)
                    pe.wait_ge(hid_ready, 2 * it + (e + 1))
                    mm = transposes(ps[6], P, [hid[:, f * P:(f + 1) * P] for f in range(4)])
                    mm.then_inc(hid_tp, 1)
                    if e == 0:
                        scatter(1, 1).then_inc(scattered, 1)
                    if e == 0:
                        mm = transposes(ps[4], P, [pick[:, b, x, :].bitcast(F32) for x in range(2) for b in range(TB)])
                        mm.then_inc(put_tp, 1)
                        for x in range(2):
                            for b in range(TB):
                                mm = pe.matmul(ps[5][:, x:x + 1], pick[:, b, x, :].bitcast(F32), combs[:, it, b, x:x + 1],
                                               start=b == 0, stop=b == 1)
                        mm.then_inc(comb_mm, 1)
                    else:
                        pe.wait_ge(pick_ready, it + 2)
                        for r in range(3):
                            gather_round(4 * it + 4, r)
                        scatter(0, 1).then_inc(scattered, 1)
                        gather_round(4 * it + 4, 3)
                        pe.wait_ge(xg_lo_ready, 4 * it + 5)
                    pe.wait_ge(hid_hi_ready, 2 * it + (e + 1))
                    pe.wait_ge(hid_lo_ready, 2 * it + (e + 1))
                    for f in range(4):
                        uq = 12 * e + 8 + f
                        pe.wait_ge(ex_hi_ready, 24 * it + (uq + 1))
                        pe.wait_ge(ex_lo_ready, 24 * it + (uq + 1 + 12))
                        wh, wl = ex_hi[uq % 4], ex_lo[uq % 4]
                        for half in range(2):
                            bank = ps[6 + half][:, :]
                            pe.matmul(bank, hid_hi[:, f, :], wh[:, half, :], start=f == 0, stop=False)
                            pe.matmul(bank, hid_lo[:, f, :], wh[:, half, :], start=False, stop=False)
                            mm = pe.matmul(bank, hid_hi[:, f, :], wl[:, half, :], start=False, stop=f == 3)
                        mm.then_inc(ex_done, 1)
            pe.wait_ge(y_lo_ready, 4 * n + 2)
            for b in range(TB):
                for half in range(2):
                    for y in (y_hi, y_lo):
                        mm = pe.matmul(ps[2 * b + half][:, :], put[:, 1, b, :], y[:, half * 512:(half + 1) * 512],
                                       start=False, stop=y is y_lo, skip_group_check=True)
            mm.then_inc(moe_done, 1)

        @block.scalar
        def _(act):
            act.wait_ge(par_in, 16)
            act.activation(cond[:, :, :], par[:, C_COND:C_COND + 16].rearrange("p (k c) -> p k c", c=2), ACT.Silu)\
               .then_inc(cond_ready, 1)
            act.wait_ge(x_loaded, 16)
            act.activation(x_sq[:, 0:4, :], x_in[:, 0:4, :], ACT.Square).then_inc(sq_ready, 1)
            act.wait_ge(ms_read, 1)
            act.activation(rms_in[:, :], mean_sq[:, :], ACT.Sqrt).then_inc(rms_ready, 1)
            def hi(u):
                act.wait_ge(raw_full[u % RAW], 16 * (u // RAW + 1))
                if u >= 2:
                    act.wait_ge(unit_done, u - 1)
                m = 64 if u == U_DT else P
                act.activation(w_hi[u % 2][:, :, 0:m], raw[:, u % RAW, :, 0:m], ACT.Copy).then_inc(split_hi, 1)

            def mod_to_rows(n):
                j = ADA_ORDER[n]
                act.wait_ge(ada_mm, n + 1)
                act.activation(mod_row[:, j * 512:(j + 1) * 512], ps[1 + j][0:2, :], ACT.Copy).then_inc(mod_row_ready, 1)

            mod_to_rows(0)
            mod_to_rows(1)
            hi(0)
            mod_to_rows(2)
            act.wait_ge(xn_chain, 2)
            for k in range(KD):
                if k == 4:
                    mod_to_rows(3)
                    hi(1)
                act.wait_ge(mod_ready, 2 if k < 4 else 4)
                for half in range(2):
                    c = 1 - half
                    act.activation(u_hi[:, half, k, :], x_in[:, k, half * T:(half + 1) * T], ACT.Identity,
                                   bias=mod_col[:, k, c:c + 1], scale=gain_col[:, k, c:c + 1]).then_inc(u_hi_ready, 1)

            def out_of_psum(u):
                if u < 0:
                    return
                bank = ps[u % 2]
                act.wait_ge(unit_done, u + 1)
                if u == U_DT:
                    act.wait_ge(headrow_in, 16)
                    act.activation(dt_e[:, :], bank[0:64, :], ACT.Abs, bias=headrow[:, 0:1]).then_inc(act_dt, 1)
                elif u < U_Z:
                    t = u - U_B
                    tile = t + 16 if u < U_X else t - 8
                    n = 2 if u < U_C or u >= U_X else 1
                    if t >= 2:
                        act.wait_ge(conv_done, t - 1)
                    act.activation(conv[t % 2][:, 0:n, :], bank[:, 0:n * T].rearrange("p (a t) -> p a t", a=n), ACT.Identity,
                                   bias=c_(C_CB + tile), scale=c_(C_CW + 4 * tile + 1)).then_inc(conv_init, 1)
                elif u < U_CH:
                    act.activation(z[:, u - U_Z, :], bank[:, 0:T], ACT.Silu).then_inc(copied, 1)
                elif u < U_GATEB:
                    i = (u - U_CH) // 2
                    if (u - U_CH) % 2 == 0:
                        if i >= 2:
                            act.wait_ge(v_chain, 3 * (i - 1))
                        act.activation(v_tmp[i % 2][:, :], bank[:, 0:T], ACT.Copy).then_inc(copied, 1)
                elif U_MB <= u < U_MA:
                    act.activation(m_b[:, u - U_MB, :], bank[:, 0:T], ACT.Copy).then_inc(copied, 1)
                elif U_MA <= u < U_SC:
                    act.activation(m_a[:, u - U_MA, :], bank[:, 0:T], ACT.Copy).then_inc(copied, 1)

            def silu(t):
                u = t + U_B
                if t < 0 or u >= U_Z:
                    return
                act.wait_ge(conv_tap, 3 * t + 3)
                src = conv[t % 2]
                if u < U_C:
                    act.activation(bc[:, t, :], src[:, 0, :], ACT.Silu)
                    act.activation(bl[:, t, :], src[:, 1, :], ACT.Silu).then_inc(conv_done, 1)
                elif u < U_X:
                    act.activation(cl[:, u - U_C, :], src[:, 0, :], ACT.Silu).then_inc(conv_done, 1)
                else:
                    act.activation(xc[:, u - U_X, :], src[:, 0, :], ACT.Silu)
                    act.activation(xl[:, u - U_X, :], src[:, 1, :], ACT.Silu).then_inc(conv_done, 1)

            def gate_hi(i):
                act.wait_ge(gated, i + 1)
                act.activation(gb_hi[:, i, :], gb_tmp[i % 2][:, :], ACT.Copy).then_inc(gb_hi_ready, 1)

            def piece_out(n):
                if n is None:
                    return
                kind, g = PIECES[n]
                if kind not in BY_ACT:
                    return
                act.wait_ge(piece, n + 1)
                if kind == "tables":
                    act.activation(tok[:, :, :, :], ps[6][:, :].rearrange("p (b k h) -> p b k h", b=2, k=4), ACT.Copy)\
                       .then_inc(piece_act, 1)
                elif kind == "b_ctx":
                    act.activation(b_tok[:, 0:4, :], ps[6][:, :].rearrange("p (b k) -> p b k", b=4), ACT.Copy)
                    act.activation(b_tok[:, 4:8, :], ps[7][:, :].rearrange("p (b k) -> p b k", b=4), ACT.Copy)\
                       .then_inc(piece_act, 1)
                elif kind == "state":
                    act.activation(state[:, g, 0, :], ps[6][:, :], ACT.Copy)
                    act.activation(state[:, g, 1, :], ps[7][:, :], ACT.Copy).then_inc(piece_act, 1)
                elif kind == "x_lat":
                    act.activation(xn[g % 2][:, 0, :], ps[6][:, :], ACT.Copy)
                    act.activation(xn[g % 2][:, 1, :], ps[7][:, :], ACT.Copy).then_inc(piece_act, 1)
                else:
                    act.wait_ge(piece_dve, dve_pieces(n + 1))
                    act.activation(cb_off[g % 2][:, :, :], ps[7][:, :].rearrange("p (s k l) -> p s k l", s=2, k=2)[:, :, 1, :],
                                   ACT.Copy).then_inc(piece_act, 1)

            for u in range(U_CH):
                if u >= 2:
                    hi(u)
                out_of_psum(u - 2)
                silu(u - 3 - U_B)
                if u == U_CH - 3:
                    act.wait_ge(piece, 10)
                    act.activation(cum_r[0:64, :, :], cum[:, 2:4, :], ACT.Copy).then_inc(cum_hi_ready, 1)
                if u == U_CH - 2:
                    act.wait_ge(cum_lo_ready, 1)
                    act.dma_start(cum_rest[64:128, :, :], cum_rest[0:64, :, :]).then_inc(cum_r_in, 16)
                if u == U_CH - 1:
                    act.activation(pick2[:, :], c_(C_PICK2, 64), ACT.Copy).then_inc(cum_hi_ready, 1)
                    act.wait_ge(cum_r_in, 16)
                    act.activation(cum_r[64:128, :, :], cum_rest[64:128, :, :], ACT.Copy).then_inc(cum_hi_ready, 1)
                if u == 3:
                    act.wait_ge(act_dt, 1)
                    act.activation(dt_e[:, :], dt_e[:, :], ACT.Exp, scale=-1.0).then_inc(act_dt, 1)
                    act.activation(a_pos[:, :], headrow[:, 1:2], ACT.Exp).then_inc(act_dt, 1)
                if u == 16:
                    act.wait_ge(dve_dt, DT_REV)
                    act.activation(w_ctx[0:32, 0, :], rev[0:32, 0, :], ACT.Exp, bias=cum[0:32, 1, P - 1:P])
                    act.activation(w_ctx[0:32, 1, :], rev[0:32, 1, :], ACT.Exp).then_inc(act_dt, 1)
                    act.activation(w_ctx[32:64, 1, :], rev[32:64, 1, :], ACT.Exp, bias=cum[32:64, 0, 0:1])
                    act.activation(w_ctx[32:64, 0, :], rev[32:64, 0, :], ACT.Exp).then_inc(act_dt, 1)
                    act.activation(dec_t[0:32, 0, :], cum[0:32, 2, :], ACT.Exp)
                    act.activation(dec_t[0:32, 1, :], cum[0:32, 3, :], ACT.Exp, bias=cum[0:32, 2, P - 1:P]).then_inc(act_dt, 1)
                    act.activation(dec_t[32:64, 1, :], cum[32:64, 3, :], ACT.Exp).then_inc(act_dt, 1)
                    act.activation(dec_t[32:64, 0, :], cum[32:64, 2, :], ACT.Exp, bias=cum[32:64, 3, 0:1]).then_inc(act_dt, 1)
                piece_out(piece_at_unit(u - 1))

            def decays(h):
                e = dec[h % 2]
                act.wait_ge(expo_ready, h + 1)
                if h >= 2:
                    act.wait_ge(mix_ready, h - 1)
                rows = ps[2 + h % 2]
                act.activation(e[:, 0:2, :], expo[:, :, :], ACT.Exp)
                act.activation(e[:, 2, :], rows[:, P:2 * P], ACT.Exp, bias=tok[:, 0, 2, h:h + 1])
                act.activation(e[:, 3, :], rows[:, T:T + P], ACT.Exp, bias=tok[:, 1, 2, 32 + h:33 + h]).then_inc(dec_ready, 1)

            def gate_y(t):
                act.wait_ge(gy_made, t + 1)
                act.activation(gg_hi[:, t, :], xl[:, t, :], ACT.Copy, scale=c_(C_SSDN + t)).then_inc(gg_hi_ready, 1)

            def units_of_step(s):
                for u in range(first_unit_of_step(s), first_unit_of_step(s + 1)):
                    hi(u)
                    out_of_psum(u - 2)
                    if U_GATEB + 3 <= u < U_MB + 3:
                        gate_hi(u - 3 - U_GATEB)

            units_of_step(0)
            for s in range(HEADS + 5):
                piece_out(piece_at_unit(U_CH - 1) if s == 0 else piece_at_step(s - 1))
                units_of_step(s + 1)
                if s < HEADS:
                    decays(s)
                if s == HEADS - 1:
                    for u in (U_SC, U_SC + 1):
                        hi(u)
                        out_of_psum(u - 2)
                    act.wait_ge(copied, 40)
                    act.activation(m_b[:, :, :], m_b[:, :, :], ACT.Sigmoid).then_inc(sig_ready, 1)
                if s == HEADS + 2:
                    hi(U_SC + 2)
                if s >= 5 and s % 2 == 1:
                    gate_y(tiles_gated(s - 1) - 1)
            for u in range(U_SC + 3, U_SSD):
                hi(u)
                if u == U_SC + 3:
                    act.activation(m_a[:, :, :], m_a[:, :, :], ACT.Sigmoid).then_inc(sig_ready, 1)
            hi(U_SSD)
            act.wait_ge(ms2_ready, 1)
            act.activation(rms2[:, :], rms2[:, :], ACT.Sqrt).then_inc(rms2_ready, 1)
            for u in range(U_SSD + 1, U_END):
                hi(u)
                if u >= U_SSD + 4 and (u - U_SSD) % 2 == 0 and (u - U_SSD - 4) // 2 < KD:
                    n = (u - U_SSD - 4) // 2
                    act.wait_ge(merge_made, n + 1)
                    act.activation(m_hi[:, n, :], merged[n % 2][:, :], ACT.Copy).then_inc(m_hi_ready, 1)
            for b in range(TB):
                act.wait_ge(h_ready, 2 * b + 2)
                act.activation(u2[:, b, :], h[:, b, :], ACT.Square, accum_out=stat[:, b:b + 1]).then_inc(h_sq, 1)
                act.wait_ge(h_ms, 2 * b + 1)
                act.activation(stat[:, 2 + b:3 + b], stat[:, 2 + b:3 + b], ACT.Sqrt).then_inc(h_rms, 1)
            for b in range(TB):
                act.wait_ge(u2_tp, b + 1)
                for i in range(2 - b):
                    act.activation(u2_t[:, 4 * i:4 * i + 4, b * P:(b + 1) * P],
                                   ps[(0, 6)[b] + i][:, :].rearrange("p (k t) -> p k t", k=4), ACT.Copy).then_inc(u2_t_act, 1)
                act.activation(u2_hi[:, b, :], u2[:, b, :], ACT.Copy).then_inc(u2_hi_ready, 1)
            def ex_split(it, q):
                act.wait_ge(ex_full[q % 12 // 4], 32 * it + 16 * (q // 12 + 1))
                act.wait_ge(ex_done, 24 * it + (q + 1))
                r = q % 4
                act.activation(ex_hi[r][:, :, :], ex_raw[q % 12 // 4][:, 2 * r:2 * r + 2, :], ACT.Copy).then_inc(ex_hi_ready, 1)

            for q in range(3):
                ex_split(0, q)
            act.wait_ge(logits_done, 1)
            act.activation(score[:, :, :], ps[2][:, 0:2 * NE].rearrange("p (b e) -> p b e", b=TB), ACT.Sigmoid)\
               .then_inc(score_ready, 1)

            def y_out(e, done, index):
                act.wait_ge(ex_done, done)
                act.wait_ge(scattered, index + 1)
                for half in range(2):
                    act.activation(y_hi[:, half * 512:(half + 1) * 512], ps[6 + half][:, :], ACT.Copy,
                                   scale=comb_slot[:, e:e + 1]).then_inc(y_hi_ready, 1)

            def gather_out(first):
                for r in range(4):
                    act.wait_ge(gathered, first + (r + 1))
                    act.activation(xg_hi[:, 2 * r:2 * r + 2, :], ps[(7, 4, 5, 4)[r]][:, :].rearrange("p (k t) -> p k t", k=2),
                                   ACT.Copy).then_inc(xg_hi_ready, 1)

            gather_out(0)
            act.wait_ge(route, ROUTE_N)
            n = act.value_load(n_iter[0:1, 0:1], min_val=8, max_val=16)

            def pair(it, first):
                for q in range(0 if first else 3):
                    ex_split(it, q)
                act.wait_ge(zeros_made, 3)
                act.wait_ge(xg_lo_ready, 4 * it + 4)
                y_out(1, 24 * it + 4, 2 * it)
                for e in range(2):
                    for q in range(3, 8):
                        ex_split(it, 12 * e + q)
                    act.wait_ge(ex_done, 24 * it + (12 * e + 8))
                    act.activation(act_g[:, :], ps[4][:, :], ACT.Silu).then_inc(act_g_ready, 1)
                    for q in range(8, 12):
                        ex_split(it, 12 * e + q)
                    act.wait_ge(hid_tp, 2 * it + (e + 1))
                    act.activation(hid_hi[:, :, :], ps[6][:, :].rearrange("p (f t) -> p f t", f=4), ACT.Copy)\
                       .then_inc(hid_hi_ready, 1)
                    if e == 0:
                        act.wait_ge(put_tp, it + 1)
                        act.activation(put[:, :, :, :], ps[4][:, :].rearrange("p (x b t) -> p x b t", x=2, b=TB), ACT.Copy)\
                           .then_inc(put_ready, 1)
                        for q in range(12, 15):
                            ex_split(it, q)
                        act.wait_ge(comb_ready, it + 1)
                        y_out(0, 24 * it + 16, 2 * it + 1)
                    else:
                        gather_out(4 * it + 4)
            pair(0, True)
            with act.Fori(1, n) as it:
                pair(it, False)
            y_out(1, 24 * n + 4, 2 * n)
            for b in range(TB):
                act.wait_ge(fin, 4 * b + 4)
                act.activation(x_nat[:, b, :], result[:, b, :], ACT.Square, accum_out=stat[:, b:b + 1]).then_inc(fin_sq, 1)
                act.wait_ge(fin, 4 * TB + 3 * b + 1)
                act.activation(stat[:, 2 + b:3 + b], stat[:, 2 + b:3 + b], ACT.Sqrt).then_inc(fin_rms, 1)

        @block.vector
        def _(dve):
            dve.sem_inc(ex_lo_ready, 12)
            dve.wait_ge(par_in, 16)
            dve.wait_ge(x_loaded, 16)
            dve.tensor_tensor(x_sq[:, 4:8, :], x_in[:, 4:8, :], x_in[:, 4:8, :], ALU.mult).then_inc(sq_sum, 1)
            dve.wait_ge(sq_ready, 1)
            for i, n in enumerate((4, 2, 1)):
                dve.wait_ge(sq_sum, i + 1)
                dve.tensor_tensor(x_sq[:, 0:n, :], x_sq[:, 0:n, :], x_sq[:, n:2 * n, :], ALU.add).then_inc(sq_sum, 1)
            dve.wait_ge(ms_done, 1)
            dve.tensor_scalar(mean_sq[:, :], ps[0][:, :], 1.0 / D, EPS, ALU.mult, ALU.add).then_inc(ms_read, 1)
            dve.wait_ge(rms_ready, 1)
            dve.reciprocal(rstd_in[:, :], rms_in[:, :]).then_inc(xn_chain, 1)
            dve.wait_ge(x_loaded, 16)
            dve.wait_ge(sq_ready, 1)
            dve.wait_ge(xn_chain, 1)
            dve.tensor_tensor(x_in[:, :, :], x_in[:, :, :], rstd_in[:, :].unsqueeze(1).to_broadcast([P, KD, 2 * T]), ALU.mult)\
               .then_inc(xn_chain, 1)
            dve.wait_ge(cond_ready, 1)
            dve.tensor_copy(cond_keep[:, :], cond[:, :, 0]).then_inc(xn_chain, 1)
            def lo(u):
                dve.wait_ge(split_hi, u + 1)
                if u >= 2:
                    dve.wait_ge(unit_done, u - 1)
                m = 64 if u == U_DT else P
                dve.tensor_tensor(w_lo[u % 2][:, :, 0:m], raw[:, u % RAW, :, 0:m], w_hi[u % 2][:, :, 0:m].bitcast(F32),
                                  ALU.subtract).then_inc(split_lo, 1)

            def modulation(half):
                def part(ap):
                    return ap.rearrange("p (s h k) c -> p s h k c", s=2, h=2)[:, :, half]

                dve.wait_ge(mod_tp, half + 1)
                dve.tensor_tensor(part(mod_col[:, :, :]), part(ps[5][:, 0:32].rearrange("p (t c) -> p t c", c=2)),
                                  part(par[:, C_BADA:C_BADA + 16].unsqueeze(2).to_broadcast([P, 16, 2])), ALU.add)\
                   .then_inc(mod_ready, 1)
                dve.wait_ge(mod_ready, 2 * half + 1)
                r = slice(4 * half, 4 * half + 4)
                dve.scalar_tensor_tensor(gain_col[:, r, :], mod_col[:, 8 + 4 * half:12 + 4 * half, :], 1.0,
                                         par[:, C_NMIX + 4 * half:C_NMIX + 4 * half + 4].unsqueeze(2).to_broadcast([P, 4, 2]),
                                         ALU.add, ALU.mult).then_inc(mod_ready, 1)
                dve.wait_ge(mod_ready, 2 * half + 2)

            modulation(0)
            lo(0)
            for k in range(KD):
                if k == 4:
                    lo(1)
                    modulation(1)
                dve.tensor_scalar(x_sq[:, k, T:], x_in[:, k, T:], gain_col[:, k, 0:1], mod_col[:, k, 0:1], ALU.mult, ALU.add)\
                   .then_inc(u_lat, 1)
                dve.wait_ge(u_lat, k + 1)
                dve.wait_ge(u_ctx, k + 1)
                dve.wait_ge(u_hi_ready, 2 * k + 2)
                dve.tensor_tensor(u_lo[:, :, k, :], x_sq[:, k, :].rearrange("p (a t) -> p a t", a=2),
                                  u_hi[:, :, k, :].bitcast(F32), ALU.subtract).then_inc(u_lo_ready, 1)

            def out_of_psum(u):
                if u < 0:
                    return
                bank = ps[u % 2]
                if u == U_DT:
                    dve.wait_ge(act_dt, 1)
                    dve.tensor_scalar(dt_r[:, :], bank[0:64, :], headrow[:, 0:1], 0.0, ALU.add, ALU.max).then_inc(dt_read, 1)
                elif u < U_Z:
                    t = u - U_B
                    tile = t + 16 if u < U_X else t - 8
                    n = 2 if u < U_C or u >= U_X else 1
                    dve.wait_ge(conv_init, t + 1)
                    src = bank[:, 0:n * T].rearrange("p (a t) -> p a t", a=n)
                    acc = conv[t % 2][:, 0:n, :]
                    for i, (tap, o, s, w) in enumerate(((0, 1, 0, T - 1), (2, 0, 1, T - 1), (3, 0, 2, T - 2))):
                        if i:
                            dve.wait_ge(conv_tap, 3 * t + i)
                        op = dve.scalar_tensor_tensor(acc[:, :, o:o + w], src[:, :, s:s + w], c_(C_CW + 4 * tile + tap),
                                                      acc[:, :, o:o + w], ALU.mult, ALU.add)
                        op.then_inc(conv_tap, 1)
                elif U_CH <= u < U_GATEB and (u - U_CH) % 2 == 1:
                    i = (u - U_CH) // 2
                    v = v_tmp[i % 2]
                    dve.wait_ge(unit_done, u + 1)
                    dve.wait_ge(copied, 16 + i + 1)
                    dve.tensor_tensor(v[:, :], v[:, :], bank[:, 0:T], ALU.mult).then_inc(v_made, 1)
                    dve.wait_ge(v_made, i + 1)
                    vg = v[:, :].rearrange("p (r w) -> p r w", w=64)
                    og = vc[:, i, :].rearrange("p (r w) -> p r w", w=64)
                    dve.tensor_scalar(vc[:, i, :], v[:, :], c_(C_SCW + 3 * i + 1), None, ALU.mult).then_inc(v_chain, 1)
                    dve.wait_ge(v_chain, 3 * i + 1)
                    dve.scalar_tensor_tensor(og[:, :, 1:64], vg[:, :, 0:63], c_(C_SCW + 3 * i), og[:, :, 1:64],
                                             ALU.mult, ALU.add).then_inc(v_chain, 1)
                    dve.wait_ge(v_chain, 3 * i + 2)
                    dve.scalar_tensor_tensor(og[:, :, 0:63], vg[:, :, 1:64], c_(C_SCW + 3 * i + 2), og[:, :, 0:63],
                                             ALU.mult, ALU.add).then_inc(v_chain, 1)
                elif U_GATEB <= u < U_MB:
                    i = u - U_GATEB
                    dve.wait_ge(unit_done, u + 1)
                    if i >= 2:
                        dve.wait_ge(gb_lo_ready, i - 1)
                    dve.wait_ge(v_chain, 3 * i + 3)
                    dve.tensor_tensor(gb_tmp[i % 2][:, :], vc[:, i, :], bank[:, 0:T], ALU.mult).then_inc(gated, 1)

            def gate_lo(i):
                dve.wait_ge(gb_hi_ready, i + 1)
                dve.tensor_tensor(gb_lo[:, i, :], gb_tmp[i % 2][:, :], gb_hi[:, i, :].bitcast(F32), ALU.subtract)\
                   .then_inc(gb_lo_ready, 1)

            def softplus(step):
                n = [0]

                def chain(op):
                    op.then_inc(dve_dt, 1)
                    n[0] += 1
                    dve.wait_ge(dve_dt, DT_AT[step] + n[0])

                if step == 0:
                    dve.wait_ge(act_dt, 3)
                    chain(dve.tensor_scalar(dt_t[:, :], dt_e[:, :], 2.0, None, ALU.add))
                    chain(dve.reciprocal(dt_t[:, :], dt_t[:, :]))
                    chain(dve.tensor_tensor(dt_t[:, :], dt_t[:, :], dt_e[:, :], ALU.mult))
                    chain(dve.tensor_tensor(dt_t2[:, :], dt_t[:, :], dt_t[:, :], ALU.mult))
                elif step == 1:
                    chain(dve.tensor_scalar(dt_q[:, :], dt_t2[:, :], LOG1P[7], None, ALU.mult))
                    for j in (6, 5, 4):
                        chain(dve.scalar_tensor_tensor(dt_q[:, :], dt_q[:, :], LOG1P[j], dt_t2[:, :], ALU.add, ALU.mult))
                elif step == 2:
                    for j in (3, 2, 1):
                        chain(dve.scalar_tensor_tensor(dt_q[:, :], dt_q[:, :], LOG1P[j], dt_t2[:, :], ALU.add, ALU.mult))
                    chain(dve.scalar_tensor_tensor(dt_q[:, :], dt_q[:, :], 1.0, dt_t[:, :], ALU.add, ALU.mult))
                elif step == 3:
                    dve.wait_ge(dt_read, 1)
                    flat = dt[:, :, :].rearrange("p c l -> p (c l)")
                    chain(dve.scalar_tensor_tensor(flat, dt_q[:, :], 2.0, dt_r[:, :], ALU.mult, ALU.add))
                    chain(dve.tensor_scalar(dt_q[:, :], flat, a_pos[:, 0:1], -1.0, ALU.mult, ALU.mult))
                elif step in (4, 5):
                    d = step - 4
                    r = slice(32 * d, 32 * d + 32)
                    q = dt_q[:, :].rearrange("p (c l) -> p c l", l=P)
                    way = slice(None) if d == 0 else slice(None, None, -1)
                    for c in range(4):
                        chain(dve.tensor_tensor_scan(cum[r, c, way], q[r, c, way], q[r, c, way], 0.0, ALU.add, ALU.bypass))
                elif step == 6:
                    for d in range(2):
                        r = slice(32 * d, 32 * d + 32)
                        end = P - 1 if d == 0 else 0
                        for c in range(4):
                            chain(dve.tensor_scalar(rev[r, c, :], cum[r, c, :], cum[r, c, end:end + 1], -1.0,
                                                    ALU.subtract, ALU.mult))
                else:
                    dve.wait_ge(act_dt, 8)
                    chain(dve.tensor_tensor(coef_t[:, :, :], w_ctx[:, :, :], dt[:, 0:2, :], ALU.mult))

            def ada_half(i):
                j = i // 2
                if i == 0:
                    dve.wait_ge(u_lo_ready, KD)
                dve.wait_ge(wa_full[j % 2], 16 * (j // 2 + 2))
                for k in range(4 * (i % 2), 4 * (i % 2) + 4):
                    src = wa[j % 2][:, k, :]
                    if k == 0:
                        op = dve.tensor_scalar(ada_sum[:, j, :], src, cond_keep[:, 0:1], None, ALU.mult)
                    else:
                        dve.wait_ge(ada_acc, 8 * j + k)
                        op = dve.scalar_tensor_tensor(ada_sum[:, j, :], src, cond_keep[:, k:k + 1], ada_sum[:, j, :],
                                                      ALU.mult, ALU.add)
                    op.then_inc(ada_acc, 1)

            def ada_out(j):
                dve.wait_ge(ada_summed, j + 1)
                if j == 0:
                    dve.wait_ge(b_row_in, 16)
                r = b_row[:, j * 512:(j + 1) * 512]
                dve.tensor_tensor(r, ps[2 + j % 2][0:1, :], r,
                                  ALU.add).then_inc(ada_row_ready, 1)

            def piece_out(n):
                if n is None:
                    return
                kind, g = PIECES[n]
                if kind not in BY_DVE:
                    return
                dve.wait_ge(piece, n + 1)
                if kind == "tables":
                    dve.tensor_copy(coef[:, :, :], ps[7][:, 0:P].rearrange("p (b h) -> p b h", b=2)).then_inc(piece_dve, 1)
                elif kind == "x_ctx":
                    for b in range(2):
                        for d in range(2):
                            op = dve.tensor_tensor(
                                xw[:, b, d, :].rearrange("p (h w) -> p h w", w=64), ps[6 + b][:, :].rearrange("p (h w) -> p h w", w=64),
                                coef[:, b, 32 * d + 8 * g:32 * d + 8 * g + 8].unsqueeze(2).to_broadcast([P, 8, 64]), ALU.mult)
                    op.then_inc(piece_dve, 1)
                elif kind == "cb":
                    diag = ps[7][:, :].rearrange("p (s k l) -> p s k l", s=2, k=2)[:, :, 0, :]
                    dve.tensor_tensor(cb_up[g % 2][:, :, :], diag, c_(C_UP, P).unsqueeze(1).to_broadcast([P, 2, P]), ALU.mult)
                    dve.tensor_tensor(cb_lo[g % 2][:, :, :], diag, c_(C_LO, P).unsqueeze(1).to_broadcast([P, 2, P]), ALU.mult)\
                       .then_inc(piece_dve, 1)
                else:
                    gg, l = g // 2, g % 2
                    y = yi[gg % 2][:, l, :]
                    n_c = 2 * (2 * gg + l)
                    if n_c == 0:
                        dve.wait_ge(ada_stored, 16)

                    def by(d):
                        return tok[:, l, 3, 32 * d + 8 * gg:32 * d + 8 * gg + 8].unsqueeze(2).to_broadcast([P, 8, 64])

                    def heads(ap):
                        return ap.rearrange("p (h w) -> p h w", w=64)

                    dve.tensor_tensor(heads(y), heads(ps[6][:, :]), by(0), ALU.mult).then_inc(carry_chain, 1)
                    dve.tensor_tensor(heads(yi_tmp[:, :]), heads(ps[7][:, :]), by(1), ALU.mult).then_inc(carry_chain, 1)
                    dve.wait_ge(carry_chain, n_c + 2)
                    dve.tensor_tensor(y, y, yi_tmp[:, :], ALU.add).then_inc(piece_dve, 1)

            for u in range(U_CH):
                if u == U_Z:
                    dve.wait_ge(split_lo, U_Z)
                if u >= U_Z:
                    lo(u)
                out_of_psum(u - 2)
                if U_X <= u < U_Z:
                    ada_half(u - U_X)
                for step in SOFTPLUS_AT.get(u, ()):
                    softplus(step)
                if u == U_CH - 3:
                    dve.wait_ge(cum_hi_ready, 1)
                    dve.tensor_tensor(cum_rest[0:64, :, :], cum[:, 2:4, :], cum_r[0:64, :, :].bitcast(F32), ALU.subtract)\
                       .then_inc(cum_lo_ready, 1)
                if u == U_Z + 2:
                    for j in range(8):
                        ada_out(j)
                piece_out(piece_at_unit(u - 1))

            def exponents(h):
                g = h // 8
                rows = ps[2 + h % 2]
                dve.wait_ge(rows_done, h + 1)
                if h >= 1:
                    dve.wait_ge(dec_ready, h)
                    dve.wait_ge(wd_ready, 2 * h)
                for b in range(2):
                    dve.tensor_scalar(back[:, b, :], rows[:, T + b * P:T + (b + 1) * P], tok[:, b, 0, 32 + h:33 + h], None,
                                      ALU.subtract).then_inc(scan_chain, 1)
                for b in range(2):
                    dve.tensor_scalar(wd_tmp[:, b, :], cb_lo[g % 2][:, b, :], tok[:, b, 1, 32 + h:33 + h], None,
                                      ALU.mult).then_inc(scan_chain, 1)
                dve.wait_ge(scan_chain, 4 * h + 2)
                for b in range(2):
                    op = dve.scalar_tensor_tensor(expo[:, b, :], rows[:, b * P:(b + 1) * P], tok[:, b, 0, h:h + 1],
                                                  back[:, b, :], ALU.subtract, ALU.min)
                op.then_inc(expo_ready, 1)
                dve.wait_ge(scan_chain, 4 * h + 4)
                for b in range(2):
                    dve.scalar_tensor_tensor(wd[h % 2][:, b, :], cb_up[g % 2][:, b, :], tok[:, b, 1, h:h + 1],
                                             wd_tmp[:, b, :], ALU.mult, ALU.add).then_inc(wd_ready, 1)

            def mixing(h):
                g = h // 8
                e, m = dec[h % 2], mix[h % 2]
                dve.wait_ge(dec_ready, h + 1)
                dve.wait_ge(wd_ready, 2 * h + 2)
                if h >= 2:
                    dve.wait_ge(y_done, h - 1)
                for b in range(2):
                    dve.tensor_tensor(m[:, 3 * b, :], e[:, b, :], wd[h % 2][:, b, :], ALU.mult)
                for b in range(2):
                    op = dve.scalar_tensor_tensor(m[:, 1 + b, :], e[:, 2 + b, :], tok[:, b, 1, 32 * b + h:32 * b + h + 1],
                                                  cb_off[g % 2][:, b, :], ALU.mult, ALU.mult)
                op.then_inc(mix_ready, 1)

            def store_y(pair):
                dve.wait_ge(y_done, 2 * pair + 2)
                dve.scalar_tensor_tensor(xl[:, pair, :], xl[:, pair, :], c_(C_DSKIP + pair), ps[4 + pair % 2][:, 0:T],
                                         ALU.mult, ALU.add).then_inc(y_stored, 1)
                dve.wait_ge(y_stored, pair + 1)
                dve.wait_ge(copied, 16)
                dve.tensor_tensor(xl[:, pair, :], xl[:, pair, :], z[:, pair, :], ALU.mult).then_inc(gy_made, 1)

            def gate_y_lo(t):
                dve.wait_ge(gg_hi_ready, t + 1)
                dve.scalar_tensor_tensor(gg_lo[:, t, :], xl[:, t, :], c_(C_SSDN + t), gg_hi[:, t, :].bitcast(F32),
                                         ALU.mult, ALU.subtract).then_inc(gg_lo_ready, 1)

            next_lo = 0
            for s in range(HEADS + 5):
                for u in range(first_unit_of_step(s), first_unit_of_step(s + 1)):
                    out_of_psum(u - 2)
                    if U_GATEB + 3 <= u < U_MB + 3:
                        gate_lo(u - 3 - U_GATEB)
                piece_out(piece_at_unit(U_CH - 1) if s == 0 else piece_at_step(s - 1))
                if s < HEADS:
                    exponents(s)
                if 1 <= s <= HEADS:
                    mixing(s - 1)
                if s == HEADS:
                    dve.wait_ge(split_lo, U_SC)
                    lo(U_SC)
                    lo(U_SC + 1)
                if s >= 4 and s % 2 == 0 and (s - 4) // 2 < 16:
                    store_y((s - 4) // 2)
                for _ in range(2):
                    if s >= 22 and next_lo < tiles_gated(s) - 1:
                        if next_lo == 0:
                            dve.wait_ge(piece, len(PIECES))
                        gate_y_lo(next_lo)
                        next_lo += 1

            def branch(n):
                dve.wait_ge(unit_done, U_SC + n + 1)
                if n == 0:
                    dve.wait_ge(sig_ready, 1)
                dve.tensor_tensor(m_b[:, n, :], ps[(U_SC + n) % 2][:, 0:T], m_b[:, n, :], ALU.mult).then_inc(branch_b, 1)

            branch(0)
            lo(U_SC + 2)
            for n in range(1, 7):
                branch(n)
                lo(U_SC + 2 + n)
                if n == 1:
                    for t in range(next_lo, 16):
                        gate_y_lo(t)
            branch(7)
            dve.wait_ge(ssq_done, 1)
            dve.tensor_scalar(rms2[:, :], ps[6][:, 0:T], 1.0 / INNER, EPS, ALU.mult, ALU.add).then_inc(ms2_ready, 1)
            dve.wait_ge(rms2_ready, 1)
            dve.reciprocal(rstd2[:, :], rms2[:, :]).then_inc(ma_scaled, 1)
            dve.wait_ge(sig_ready, 2)
            dve.wait_ge(ma_scaled, 1)
            dve.tensor_tensor(m_a[:, :, :], m_a[:, :, :], rstd2[:, :].unsqueeze(1).to_broadcast([P, KD, T]), ALU.mult)\
               .then_inc(ma_scaled, 1)

            def merge(n):
                dve.wait_ge(unit_done, U_SSD + 2 * n + 2)
                if n == 0:
                    dve.wait_ge(ma_scaled, 2)
                    dve.wait_ge(branch_b, KD)
                if n >= 2:
                    dve.wait_ge(m_lo_ready, n - 1)
                m = merged[n % 2][:, :]
                dve.tensor_tensor(m, ps[n % 2][:, 0:T], m_a[:, n, :], ALU.mult).then_inc(merge_chain, 1)
                dve.wait_ge(merge_chain, n + 1)
                dve.tensor_tensor(m, m, m_b[:, n, :], ALU.add).then_inc(merge_made, 1)

            def merge_lo(n):
                dve.wait_ge(m_hi_ready, n + 1)
                dve.tensor_tensor(m_lo[:, n, :], merged[n % 2][:, :], m_hi[:, n, :].bitcast(F32), ALU.subtract)\
                   .then_inc(m_lo_ready, 1)

            for u in range(U_SSD + 1, U_END):
                lo(u)
                n, odd = (u - U_SSD - 2) // 2, (u - U_SSD) % 2
                if n >= 0 and odd and n < KD:
                    merge(n)
                if n >= 1 and not odd and n <= KD:
                    merge_lo(n - 1)
            dve.wait_ge(norm_rows_in, 16)
            dve.wait_ge(mod_rest_in, 16)
            dve.scalar_tensor_tensor(norm_rows[:, 0, :], mod_rest[:, 2, :], 1.0, norm_rows[:, 0, :], ALU.add, ALU.mult)\
               .then_inc(nf_made, 1)
            dve.wait_ge(unit_done, U_END)
            dve.wait_ge(x_nat_in, 16)

            def halves(half):
                return slice(half * 512, (half + 1) * 512)

            for b in range(TB):
                for half in range(2):
                    dve.tensor_tensor(h[:, b, halves(half)], ps[2 + 2 * b + half][:, :], mod_rest[:, 0, halves(half)],
                                      ALU.mult).then_inc(h_scaled, 1)
                for half in range(2):
                    dve.wait_ge(h_scaled, 2 * b + half + 1)
                    dve.tensor_tensor(h[:, b, halves(half)], h[:, b, halves(half)], x_nat[:, b, halves(half)],
                                      ALU.add).then_inc(h_ready, 1)
            dve.wait_ge(nf_made, 1)
            for b in range(TB):
                r = stat[:, 2 + b:3 + b]
                dve.wait_ge(h_sq, b + 1)
                dve.tensor_scalar(r, stat[:, b:b + 1], 1.0 / D, EPS, ALU.mult, ALU.add).then_inc(h_ms, 1)
                dve.wait_ge(h_rms, b + 1)
                dve.reciprocal(r, r).then_inc(h_ms, 1)
                dve.wait_ge(h_ms, 2 * b + 2)
                dve.scalar_tensor_tensor(u2[:, b, :], h[:, b, :], stat[:, 2 + b:3 + b], norm_rows[:, 0, :], ALU.mult, ALU.mult)\
                   .then_inc(u2_chain, 1)
                dve.wait_ge(u2_chain, 2 * b + 1)
                dve.tensor_tensor(u2[:, b, :], u2[:, b, :], mod_rest[:, 1, :], ALU.add).then_inc(u2_chain, 1)
            dve.wait_ge(u2_tp, 2)
            dve.tensor_copy(u2_t[:, 4:8, P:], ps[7][:, :].rearrange("p (k t) -> p k t", k=4)).then_inc(u2_t_dve, 1)
            dve.wait_ge(h_ready, 2 * TB)
            dve.memset(zero_r[:, :].bitcast(F32), 0.0).then_inc(zeros_made, 1)
            dve.memset(put[:, :, :, :].bitcast(F32), 0.0).then_inc(zeros_made, 1)
            dve.memset(comb_slot[:, :], 0.0).then_inc(zeros_made, 1)
            for b in range(TB):
                dve.wait_ge(u2_hi_ready, b + 1)
                dve.tensor_tensor(u2_lo[:, b, :], u2[:, b, :], u2_hi[:, b, :].bitcast(F32), ALU.subtract).then_inc(u2_lo_ready, 1)

            def ex_lo_(it, q):
                r = q % 4
                dve.wait_ge(ex_hi_ready, 24 * it + (q + 1))
                dve.tensor_tensor(ex_lo[r][:, :, :], ex_raw[q % 12 // 4][:, 2 * r:2 * r + 2, :], ex_hi[r][:, :, :].bitcast(F32),
                                  ALU.subtract).then_inc(ex_lo_ready, 1)

            for q in range(3):
                ex_lo_(0, q)
            n_route = [0]

            def step(op):
                op.then_inc(route, 1)
                n_route[0] += 1
                dve.wait_ge(route, n_route[0])

            def ranks(values, n, to):
                v_j = values.unsqueeze(2).to_broadcast([P, n, 4, 4])
                v_i = values.unsqueeze(3).to_broadcast([P, n, 4, 4])
                gt, ge = cmp_gt[:, 0:n], cmp_ge[:, 0:n]

                def mask(m, c):
                    f = m.rearrange("p c i j -> p c (i j)")
                    step(dve.tensor_tensor(f, f, c_(c, 16).unsqueeze(1).to_broadcast([P, n, 16]), ALU.mult))

                step(dve.tensor_tensor(gt, v_j, v_i, ALU.is_gt))
                step(dve.tensor_tensor(ge, v_j, v_i, ALU.is_ge))
                mask(gt, C_NTRI)
                mask(ge, C_TRI)
                step(dve.tensor_tensor(gt, gt, ge, ALU.add))
                step(dve.tensor_reduce(to, gt, AX_X, ALU.add))

            def by4(ap):
                return ap.rearrange("p b (g e) -> p (b g) e", e=4)

            dve.wait_ge(score_ready, 1)
            dve.wait_ge(b_rt_in, 16)
            step(dve.tensor_tensor(sel[:, :, :], score[:, :, :], b_rt[:, :].unsqueeze(1).to_broadcast([P, TB, NE]), ALU.add))
            ranks(by4(sel[:, :, :]), 8, rank[:, :, :])
            step(dve.tensor_scalar(top2[:, :, :], rank[:, :, :], 1.5, None, ALU.is_lt))
            step(dve.tensor_tensor(sel_top[:, :, :], top2[:, :, :], by4(sel[:, :, :]), ALU.mult))
            step(dve.tensor_reduce(g_score[:, :], sel_top[:, :, :], AX_X, ALU.add))
            ranks(g_score[:, :].rearrange("p (b g) -> p b g", b=TB), TB, g_rank[:, :].rearrange("p (b g) -> p b g", b=TB))
            step(dve.tensor_scalar(g_rank[:, :], g_rank[:, :], 0.5, None, ALU.is_lt))
            step(dve.tensor_tensor(by4(chosen[:, :, :]), top2[:, :, :], g_rank[:, :].unsqueeze(2).to_broadcast([P, 8, 4]),
                                   ALU.mult))
            assert n_route[0] == ROUTE_CHOSEN
            step(dve.tensor_tensor(comb[:, :, :], score[:, :, :], chosen[:, :, :], ALU.mult))
            step(dve.tensor_reduce(stat[:, 4:6], comb[:, :, :], AX_X, ALU.add))
            step(dve.reciprocal(stat[:, 4:6], stat[:, 4:6]))
            step(dve.tensor_tensor(comb[:, :, :], comb[:, :, :], stat[:, 4:6].unsqueeze(2).to_broadcast([P, TB, NE]), ALU.mult))

            def pairs(ap):
                return ap.rearrange("p b (i x) -> p i b x", x=2)

            for k in range(2):
                step(dve.tensor_copy(combs[:, 8 * k:8 * k + 8, :, :], pairs(comb[:, :, :])))
            def make_pick(i):
                dve.tensor_tensor(pick[:, :, :, :].rearrange("p b x t -> p (b x) t"),
                                  c_(C_IOTA, P).unsqueeze(1).to_broadcast([P, 4, P]),
                                  slots[:, i, :, :].rearrange("p b x -> p (b x)").unsqueeze(2).to_broadcast([P, 4, P]),
                                  ALU.is_equal).then_inc(pick_ready, 1)

            dve.wait_ge(positions, 1)
            step(dve.tensor_tensor(slot[:, :, :], ps[3][:, 0:2 * NE].rearrange("p (b e) -> p b e", b=TB), chosen[:, :, :], ALU.mult))
            step(dve.tensor_scalar(slots[:, 0:8, :, :], pairs(slot[:, :, :]), -1.0, None, ALU.add))
            make_pick(0)
            step(dve.tensor_reduce(stat[0:1, 6:7], ps[3][0:1, 2 * NE:3 * NE], AX_X, ALU.max))
            assert n_route[0] == ROUTE_READ
            step(dve.tensor_scalar(stat[0:1, 6:7], stat[0:1, 6:7], float(P), 8.0, ALU.is_gt, ALU.mult))
            step(dve.tensor_scalar(n_iter[:, 0:1], stat[0:1, 6:7], 8.0, None, ALU.add))
            step(dve.tensor_scalar(slots[:, 8:16, :, :], pairs(slot[:, :, :]), -1.0 - P, None, ALU.add))
            step(dve.memset(slots[:, 16, :, :], -1.0))
            assert n_route[0] == ROUTE_N

            def y_rest(e, index):
                for half in range(2):
                    dve.wait_ge(y_hi_ready, 2 * index + (half + 1))
                    dve.scalar_tensor_tensor(y_lo[:, halves(half)], ps[6 + half][:, :], comb_slot[:, e:e + 1],
                                             y_hi[:, halves(half)].bitcast(F32), ALU.mult, ALU.subtract).then_inc(y_lo_ready, 1)

            def gather_rest(first):
                for r in range(4):
                    dve.wait_ge(xg_hi_ready, first + (r + 1))
                    dve.tensor_tensor(xg_lo[:, 2 * r:2 * r + 2, :], ps[(7, 4, 5, 4)[r]][:, :].rearrange("p (k t) -> p k t", k=2),
                                      xg_hi[:, 2 * r:2 * r + 2, :].bitcast(F32), ALU.subtract).then_inc(xg_lo_ready, 1)

            dve.wait_ge(zeros_made, 3)
            gather_rest(0)
            n = dve.value_load(n_iter[0:1, 0:1], min_val=8, max_val=16)

            def pair(it, first):
                for q in range(0 if first else 3):
                    ex_lo_(it, q)
                y_rest(1, 2 * it)
                for e in range(2):
                    for q in range(3, 10):
                        ex_lo_(it, 12 * e + q)
                    dve.wait_ge(ex_done, 24 * it + (12 * e + 12))
                    dve.wait_ge(act_g_ready, 2 * it + (e + 1))
                    dve.tensor_tensor(hid[:, :], act_g[:, :], ps[5][:, :], ALU.mult).then_inc(hid_ready, 1)
                    ex_lo_(it, 12 * e + 10)
                    dve.wait_ge(hid_hi_ready, 2 * it + (e + 1))
                    dve.tensor_tensor(hid_lo[:, :, :], ps[6][:, :].rearrange("p (f t) -> p f t", f=4),
                                      hid_hi[:, :, :].bitcast(F32), ALU.subtract).then_inc(hid_lo_ready, 1)
                    ex_lo_(it, 12 * e + 11)
                    if e == 0:
                        dve.wait_ge(comb_mm, it + 1)
                        dve.tensor_copy(comb_slot[:, :], ps[5][:, 0:2]).then_inc(comb_ready, 1)
                        make_pick(it + 1)
                        for q in range(12, 15):
                            ex_lo_(it, q)
                        dve.wait_ge(comb_ready, it + 1)
                        y_rest(0, 2 * it + 1)
                    else:
                        gather_rest(4 * it + 4)
            pair(0, True)
            with dve.Fori(1, n) as it:
                pair(it, False)
            y_rest(1, 2 * n)
            dve.wait_ge(moe_done, 1)
            for b in range(TB):
                for half in range(2):
                    dve.tensor_tensor(result[:, b, halves(half)], ps[2 * b + half][:, :], mod_rest[:, 3, halves(half)],
                                      ALU.mult).then_inc(fin, 1)
                for half in range(2):
                    dve.wait_ge(fin, 4 * b + half + 1)
                    dve.tensor_tensor(result[:, b, halves(half)], result[:, b, halves(half)], h[:, b, halves(half)],
                                      ALU.add).then_inc(fin, 1)
            for b in range(TB):
                r, n = stat[:, 2 + b:3 + b], 4 * TB + 3 * b
                dve.wait_ge(fin_sq, b + 1)
                dve.tensor_scalar(r, stat[:, b:b + 1], 1.0 / D, EPS, ALU.mult, ALU.add).then_inc(fin, 1)
                dve.wait_ge(fin_rms, b + 1)
                dve.reciprocal(r, r).then_inc(fin, 1)
                dve.wait_ge(fin, n + 2)
                dve.scalar_tensor_tensor(result[:, b, :], result[:, b, :], r, norm_rows[:, 1, :], ALU.mult, ALU.mult)\
                   .then_inc(fin, 1)

        @block.gpsimd
        def _(pool):
            pool.wait_ge(xn_chain, 2)
            for k in range(KD):
                pool.wait_ge(mod_ready, 2 if k < 4 else 4)
                pool.tensor_scalar(x_sq[:, k, 0:T], x_in[:, k, 0:T], gain_col[:, k, 1:2], mod_col[:, k, 1:2],
                                   ALU.mult, ALU.add).then_inc(u_ctx, 1)
            def square(t):
                pool.wait_ge(gy_made, t + 1)
                n = 2 * t
                if t == 0:
                    pool.tensor_tensor(sq_all[:, :], xl[:, t, :], xl[:, t, :], ALU.mult).then_inc(sq_step, 1)
                    return
                pool.wait_ge(sq_step, n - 1)
                pool.tensor_tensor(gy_sq[:, :], xl[:, t, :], xl[:, t, :], ALU.mult).then_inc(sq_step, 1)
                pool.wait_ge(sq_step, n)
                pool.tensor_tensor(sq_all[:, :], sq_all[:, :], gy_sq[:, :], ALU.add).then_inc(sq_step, 1)

            def lo(u):
                pool.wait_ge(split_lo, u)
                pool.wait_ge(split_hi, u + 1)
                pool.wait_ge(unit_done, u - 1)
                pool.tensor_tensor(w_lo[u % 2][:, :, :], raw[:, u % RAW, :, :], w_hi[u % 2][:, :, :].bitcast(F32),
                                   ALU.subtract).then_inc(split_lo, 1)

            for u in range(2, U_Z):
                lo(u)
            for s in range(HEADS + 5):
                for u in range(first_unit_of_step(s), first_unit_of_step(s + 1)):
                    lo(u)
                if s >= 5 and s % 2 == 1:
                    square(tiles_gated(s - 1) - 1)


def kernel(**inputs):
    import numpy as np
    import concourse.bacc as bacc
    from concourse.bass_utils import run_bass_kernel_spmd

    nc, arrays, _ = prepare(inputs, np, bacc)
    r = run_bass_kernel_spmd(nc, [arrays], core_ids=[0])
    return r.results[0]["out"].reshape(1, T, D)


def prepare(inputs, np, bacc):
    i = {k: np.ascontiguousarray(v) for k, v in inputs.items()}

    def cols(v):
        return v.reshape(-1, P).T

    def tiles(w):
        k, n = w.shape
        return w.reshape(k // P, P, n // P, P).transpose(2, 1, 0, 3)

    par = np.zeros((P, C_END), np.float32)
    par[:, C_COND:C_COND + 16] = np.stack([cols(i["c"][0]), cols(i["c_ctx"])], -1).reshape(P, 16)
    par[:, C_BADA:C_BADA + 16] = cols(i["b_ada"][0, :2048])
    par[:, C_NMIX:C_NMIX + 8] = cols(i["norm_mix"][0])
    par[:, C_CW:C_CW + 96] = i["ssd_conv_w"][0].reshape(4, 24, P).transpose(2, 1, 0).reshape(P, 96)
    par[:, C_CB:C_CB + 24] = cols(i["ssd_conv_b"][0])
    par[:, C_SSDN:C_SSDN + 16] = cols(i["ssd_norm"][0])
    par[:, C_SCW:C_SCW + 24] = i["sc_conv_w"][0].reshape(3, 8, P).transpose(2, 1, 0).reshape(P, 24)
    par[:, C_DSKIP:C_DSKIP + 16] = cols(np.repeat(i["ssd_d"][0], 64))
    at = np.arange(P)
    par[:, C_IDENT:C_IDENT + P] = np.eye(P)
    par[:, C_ONES:C_ONES + P] = 1
    par[:, C_UP:C_UP + P] = at[None, :] >= at[:, None]
    par[:, C_LO:C_LO + P] = at[None, :] <= at[:, None]
    par[:, C_IOTA:C_IOTA + P] = at[None, :]
    tri = (np.arange(4)[None, :] < np.arange(4)[:, None]).reshape(16)
    par[:, C_TRI:C_TRI + 16] = tri
    par[:, C_NTRI:C_NTRI + 16] = ~tri
    par[:, C_PICK2:C_PICK2 + 64] = at[:, None] % 64 == np.arange(64)[None, :]
    w_in = i["w_in"][0]
    z, x, b, c, dt, sb, sc, sh, ma, mb = np.split(w_in, [2048, 4096, 4608, 5120, 5184, 6208, 7232, 8256, 9280], 1)
    units = [tiles(b), tiles(c), tiles(x), tiles(z),
             np.stack([tiles(sc), tiles(sh)], 1).reshape(16, P, KD, P), tiles(sb), tiles(mb), tiles(ma),
             tiles(i["w_sc_out"][0]),
             i["w_ssd_out"][0].reshape(2, KD, P, KD, P).transpose(3, 0, 2, 1, 4).reshape(16, P, KD, P),
             i["w_o"][0].reshape(KD, P, KD, P)]
    tokens = np.concatenate([i["ctx"][0], i["x"][0]])
    experts = np.stack([i["w_gate"][0].reshape(NE, KD, P, 512).transpose(0, 2, 1, 3),
                        i["w_up"][0].reshape(NE, KD, P, 512).transpose(0, 2, 1, 3),
                        i["w_down"][0].reshape(NE, 4, P, D).transpose(0, 2, 1, 3).reshape(NE, P, KD, 512)], 1)
    arrays = {
        "par": par,
        "head_rows": np.stack([i["ssd_dt_bias"][0].reshape(64), i["ssd_a_log"][0].reshape(64)], 1),
        "x_t": tokens.reshape(2 * T, KD, P).transpose(2, 1, 0),
        "x": i["x"][0],
        "w_ada": i["w_ada"][0].reshape(KD, P, 12, 512).transpose(2, 1, 0, 3),
        "b_ada_rest": i["b_ada"][0, 2048:].reshape(1, 4096),
        "w_dt": dt.reshape(KD, P, 64).transpose(1, 0, 2),
        "units": np.concatenate(units),
        "w_router": i["w_router"].reshape(KD, P, NE).transpose(1, 0, 2),
        "rows": np.stack([i["norm_ffn"][0], i["final_norm"]]),
        "b_router": i["b_router"].reshape(1, NE),
        "experts": experts.reshape(3 * NE, P, KD, 512),
    }
    arrays = {k: np.ascontiguousarray(v) for k, v in arrays.items()}
    nc = bacc.Bacc("TRN2", target_bir_lowering=False, num_devices=1)
    a = {k: nc.dram_tensor(k, v.shape, F32, kind="ExternalInput").ap() for k, v in arrays.items()}
    out = nc.dram_tensor("out", (T, D), F32, kind="ExternalOutput").ap()
    scratch = nc.dram_tensor("ada_scratch", (1, 4096), F32, kind="Internal").ap()
    build(nc, a, out, scratch)
    return nc, arrays, out
```
